# Optimizing a Trainium2 kernel written in Bass

```python
import math
import jax
import jax.numpy as jnp
from jax import lax
import numpy as np

D_MODEL = 1024
BATCH = 1
SEQ = 256
DEPTH = 2

HEAD_DIM = 64
N_HEADS = D_MODEL // HEAD_DIM
A_HEADS = N_HEADS // 2
B_HEADS = N_HEADS - A_HEADS
B_KV_HEADS = max(1, B_HEADS // 4)
C_HEADS = N_HEADS
C_KV_HEADS = max(1, C_HEADS // 4)
MIX_WIDTH = N_HEADS * HEAD_DIM
A_PATTERNS = ((128, 1), (512, 4), (2048, 16))
A_BLOCK = 64
B_WINDOW = 128
B_BLOCK = 128
C_BLOCK = 128
GRID_W = 64
ROPE_THETA = 10000.0
ROPE_AXIS_DIM = HEAD_DIM // 2
ALIBI_MAX_BIAS = 8.0
RMS_EPS = 1e-6
MOE_GROUPS = 4
MOE_EXPERTS = 8
MOE_TOP_K = 2
MOE_D_FF = D_MODEL // 4
A_W = A_HEADS * HEAD_DIM
B_QW = B_HEADS * HEAD_DIM
B_KVW = B_KV_HEADS * HEAD_DIM
AB_SPLITS = (A_W, 2 * A_W, 3 * A_W, 3 * A_W + B_QW, 3 * A_W + B_QW + B_KVW)
AB_PROJ = 3 * A_W + B_QW + 2 * B_KVW
C_QW = C_HEADS * HEAD_DIM
C_KVW = C_KV_HEADS * HEAD_DIM
C_SPLITS = (C_QW, C_QW + C_KVW)
C_PROJ = C_QW + 2 * C_KVW
N_EVEN = (DEPTH + 1) // 2
N_ODD = DEPTH // 2

kernel_name = 'hybrid_dilated_window_axial_hmoe'

def _rmsnorm(x, g):
    x32 = x.astype(jnp.float32)
    y = x32 * lax.rsqrt(jnp.mean(x32 * x32, axis=-1, keepdims=True) + RMS_EPS)
    return (y * g.astype(jnp.float32)).astype(x.dtype)

def _alibi_slopes(n):
    return jnp.asarray(2.0 ** (-ALIBI_MAX_BIAS * np.arange(1, n + 1) / n), dtype=jnp.float32)

def _banded_attention(q, k, v, half_window, block, dist_scale, slopes, sink=None):
    b, L, H, hd = q.shape
    hkv = k.shape[2]
    grp = H // hkv
    nblk = -(-L // block)
    lp = nblk * block
    kw = block + 2 * half_window
    qp = jnp.pad(q, ((0, 0), (0, lp - L), (0, 0), (0, 0)))
    pad_k = ((0, 0), (half_window, lp - L + half_window), (0, 0), (0, 0))
    kp = jnp.pad(k, pad_k)
    vp = jnp.pad(v, pad_k)
    key_idx = np.arange(nblk)[:, None] * block + np.arange(kw)[None, :]
    kb = kp[:, key_idx]
    vb = vp[:, key_idx]
    qb = qp.reshape(b, nblk, block, hkv, grp, hd)
    s = jnp.einsum('bnqkgd,bnskd->bnkgqs', qb, kb, preferred_element_type=jnp.float32) * (hd ** -0.5)
    qpos = np.arange(nblk)[:, None] * block + np.arange(block)[None, :]
    kpos = key_idx - half_window
    rel = np.abs(kpos[:, None, :] - qpos[:, :, None])
    valid = (rel <= half_window) & (kpos[:, None, :] >= 0) & (kpos[:, None, :] < L)
    dist = jnp.asarray(rel, dtype=jnp.float32) * dist_scale
    slopes_kg = slopes.reshape(hkv, grp)
    s = s - slopes_kg[None, None, :, :, None, None] * dist[None, :, None, None, :, :]
    s = jnp.where(valid[None, :, None, None], s, -jnp.inf)
    m = jnp.max(s, axis=-1, keepdims=True)
    if sink is not None:
        sink_b = sink.astype(jnp.float32).reshape(hkv, grp)[None, None, :, :, None, None]
        m = jnp.maximum(m, sink_b)
    p = jnp.exp(s - m)
    l = jnp.sum(p, axis=-1, keepdims=True)
    if sink is not None:
        l = l + jnp.exp(sink_b - m)
    o = jnp.einsum('bnkgqs,bnskd->bnqkgd', p.astype(v.dtype), vb, preferred_element_type=jnp.float32)
    o = o / jnp.moveaxis(l[..., 0], -1, 2)[..., None]
    lse = jnp.moveaxis((m + jnp.log(l))[..., 0], -1, 2)
    o = o.reshape(b, lp, H, hd)[:, :L]
    lse = lse.reshape(b, lp, H)[:, :L]
    return o, lse

def _to_strided(t, dil):
    b, S, h, hd = t.shape
    return t.reshape(b, S // dil, dil, h, hd).transpose(0, 2, 1, 3, 4).reshape(b * dil, S // dil, h, hd)

def _from_strided(t, b, dil):
    bd, L = t.shape[0], t.shape[1]
    rest = t.shape[2:]
    t = t.reshape((b, dil, L) + rest)
    t = jnp.moveaxis(t, 1, 2)
    return t.reshape((b, L * dil) + rest)

def _dilated_mixture(q, k, v, slopes):
    b = q.shape[0]
    outs, lses = [], []
    for window, dil in A_PATTERNS:
        half = (window // 2) // dil
        o, lse = _banded_attention(_to_strided(q, dil), _to_strided(k, dil), _to_strided(v, dil),
                                   half, A_BLOCK, float(dil), slopes)
        outs.append(_from_strided(o, b, dil))
        lses.append(_from_strided(lse, b, dil))
    w = jax.nn.softmax(jnp.stack(lses, axis=0), axis=0)
    return jnp.sum(w[..., None] * jnp.stack(outs, axis=0), axis=0)

def _mixer_ab(h, w_in, a_qn, a_kn, b_qn, b_kn, b_sink, w_out):
    b, S, _ = h.shape
    proj = jnp.einsum('bsd,de->bse', h, w_in)
    qa, ka, va, qb, kb, vb = jnp.split(proj, AB_SPLITS, axis=-1)
    qa = _rmsnorm(qa.reshape(b, S, A_HEADS, HEAD_DIM), a_qn)
    ka = _rmsnorm(ka.reshape(b, S, A_HEADS, HEAD_DIM), a_kn)
    va = va.reshape(b, S, A_HEADS, HEAD_DIM)
    qb = _rmsnorm(qb.reshape(b, S, B_HEADS, HEAD_DIM), b_qn)
    kb = _rmsnorm(kb.reshape(b, S, B_KV_HEADS, HEAD_DIM), b_kn)
    vb = vb.reshape(b, S, B_KV_HEADS, HEAD_DIM)
    slopes = _alibi_slopes(A_HEADS + B_HEADS)
    oa = _dilated_mixture(qa, ka, va, slopes[0::2])
    ob, _ = _banded_attention(qb, kb, vb, B_WINDOW, B_BLOCK, 1.0, slopes[1::2], sink=b_sink)
    o = jnp.concatenate([oa.reshape(b, S, A_W), ob.reshape(b, S, B_QW)], axis=-1).astype(h.dtype)
    return jnp.einsum('bse,ed->bsd', o, w_out)

def _axial_rope_tables(seq_len):
    rows = seq_len // GRID_W
    row = jnp.broadcast_to(jnp.arange(rows, dtype=jnp.float32)[:, None], (rows, GRID_W)).reshape(-1)
    col = jnp.broadcast_to(jnp.arange(GRID_W, dtype=jnp.float32)[None, :], (rows, GRID_W)).reshape(-1)
    inv_freq = ROPE_THETA ** (-jnp.arange(0, ROPE_AXIS_DIM, 2, dtype=jnp.float32) / ROPE_AXIS_DIM)
    ang_r = row[:, None] * inv_freq[None, :]
    ang_c = col[:, None] * inv_freq[None, :]
    return jnp.cos(ang_r), jnp.sin(ang_r), jnp.cos(ang_c), jnp.sin(ang_c)

def _rotate(t, cos, sin):
    half = t.shape[-1] // 2
    t1, t2 = t[..., :half], t[..., half:]
    c = cos[None, :, None, :]
    s = sin[None, :, None, :]
    return jnp.concatenate([t1 * c - t2 * s, t2 * c + t1 * s], axis=-1)

def _apply_axial_rope(x, cr, sr, cc, sc):
    x32 = x.astype(jnp.float32)
    out = jnp.concatenate([_rotate(x32[..., :ROPE_AXIS_DIM], cr, sr),
                           _rotate(x32[..., ROPE_AXIS_DIM:], cc, sc)], axis=-1)
    return out.astype(x.dtype)

def _dense_blocked_attention(q, k, v):
    b, S, H, hd = q.shape
    hkv = k.shape[2]
    grp = H // hkv
    nq = S // C_BLOCK
    qb = q.reshape(b, nq, C_BLOCK, hkv, grp, hd).transpose(1, 0, 2, 3, 4, 5)

    def one_block(qblk):
        s = jnp.einsum('bqkgd,bskd->bkgqs', qblk, k, preferred_element_type=jnp.float32) * (hd ** -0.5)
        p = jax.nn.softmax(s, axis=-1)
        o = jnp.einsum('bkgqs,bskd->bqkgd', p.astype(v.dtype), v, preferred_element_type=jnp.float32)
        return o.astype(q.dtype)

    o = lax.map(one_block, qb)
    return o.transpose(1, 0, 2, 3, 4, 5).reshape(b, S, H, hd)

def _mixer_c(h, w_in, qn, kn, w_out):
    b, S, _ = h.shape
    proj = jnp.einsum('bsd,de->bse', h, w_in)
    q, k, v = jnp.split(proj, C_SPLITS, axis=-1)
    q = _rmsnorm(q.reshape(b, S, C_HEADS, HEAD_DIM), qn)
    k = _rmsnorm(k.reshape(b, S, C_KV_HEADS, HEAD_DIM), kn)
    v = v.reshape(b, S, C_KV_HEADS, HEAD_DIM)
    cr, sr, cc, sc = _axial_rope_tables(S)
    q = _apply_axial_rope(q, cr, sr, cc, sc)
    k = _apply_axial_rope(k, cr, sr, cc, sc)
    o = _dense_blocked_attention(q, k, v).reshape(b, S, C_QW)
    return jnp.einsum('bse,ed->bsd', o, w_out)

def _hier_moe(h, wg, bg, we, be, w_gate, w_up, w_down):
    b, S, d = h.shape
    xt = h.reshape(b * S, d)
    pg = jax.nn.softmax(jnp.einsum('nd,dg->ng', xt, wg, preferred_element_type=jnp.float32)
                        + bg.astype(jnp.float32), axis=-1)
    g_idx = jnp.argmax(pg, axis=-1)
    onehot_g = jax.nn.one_hot(g_idx, MOE_GROUPS, dtype=jnp.float32)
    p_grp = jnp.sum(pg * onehot_g, axis=-1)
    logits_e = jnp.einsum('nd,gde->nge', xt, we, preferred_element_type=jnp.float32) + be.astype(jnp.float32)[None]
    sel = jnp.einsum('nge,ng->ne', logits_e, onehot_g)
    pe = jax.nn.softmax(sel, axis=-1)
    top_p, top_i = lax.top_k(pe, MOE_TOP_K)
    top_p = top_p / jnp.sum(top_p, axis=-1, keepdims=True)
    w_e = jnp.sum(top_p[..., None] * jax.nn.one_hot(top_i, MOE_EXPERTS, dtype=jnp.float32), axis=1)
    comb = p_grp[:, None, None] * onehot_g[:, :, None] * w_e[:, None, :]
    y = jnp.zeros((b * S, d), jnp.float32)
    for g in range(MOE_GROUPS):
        a = jnp.einsum('nd,edf->nef', xt, w_gate[g], preferred_element_type=jnp.float32)
        u = jnp.einsum('nd,edf->nef', xt, w_up[g], preferred_element_type=jnp.float32)
        act = jax.nn.silu(a) * u * comb[:, g, :, None]
        y = y + jnp.einsum('nef,efd->nd', act.astype(xt.dtype), w_down[g], preferred_element_type=jnp.float32)
    return y.reshape(b, S, d).astype(h.dtype)

def setup_inputs(seed: int = 0) -> dict:
    key = jax.random.key(seed)
    ks = jax.random.split(key, 21)

    def nrm(k, shape, scale):
        return jax.random.normal(k, shape, jnp.float32) * scale

    def gain(k, shape):
        return 1.0 + 0.02 * jax.random.normal(k, shape, jnp.float32)

    return {
        'x': nrm(ks[0], (BATCH, SEQ, D_MODEL), 1.0),
        'mix_norm': gain(ks[1], (DEPTH, D_MODEL)),
        'ffn_norm': gain(ks[2], (DEPTH, D_MODEL)),
        'ab_w_in': nrm(ks[3], (N_EVEN, D_MODEL, AB_PROJ), D_MODEL ** -0.5),
        'a_q_norm': gain(ks[4], (N_EVEN, HEAD_DIM)),
        'a_k_norm': gain(ks[5], (N_EVEN, HEAD_DIM)),
        'b_q_norm': gain(ks[6], (N_EVEN, HEAD_DIM)),
        'b_k_norm': gain(ks[7], (N_EVEN, HEAD_DIM)),
        'b_sink': nrm(ks[8], (N_EVEN, B_HEADS), 0.5),
        'ab_w_out': nrm(ks[9], (N_EVEN, MIX_WIDTH, D_MODEL), MIX_WIDTH ** -0.5),
        'c_w_in': nrm(ks[10], (N_ODD, D_MODEL, C_PROJ), D_MODEL ** -0.5),
        'c_q_norm': gain(ks[11], (N_ODD, HEAD_DIM)),
        'c_k_norm': gain(ks[12], (N_ODD, HEAD_DIM)),
        'c_w_out': nrm(ks[13], (N_ODD, C_QW, D_MODEL), C_QW ** -0.5),
        'moe_group_w': nrm(ks[14], (DEPTH, D_MODEL, MOE_GROUPS), D_MODEL ** -0.5),
        'moe_group_b': nrm(ks[15], (DEPTH, MOE_GROUPS), 0.01),
        'moe_expert_w': nrm(ks[16], (DEPTH, MOE_GROUPS, D_MODEL, MOE_EXPERTS), D_MODEL ** -0.5),
        'moe_expert_b': nrm(ks[17], (DEPTH, MOE_GROUPS, MOE_EXPERTS), 0.01),
        'moe_w_gate': nrm(ks[18], (DEPTH, MOE_GROUPS, MOE_EXPERTS, D_MODEL, MOE_D_FF), D_MODEL ** -0.5),
        'moe_w_up': nrm(ks[19], (DEPTH, MOE_GROUPS, MOE_EXPERTS, D_MODEL, MOE_D_FF), D_MODEL ** -0.5),
        'moe_w_down': nrm(ks[20], (DEPTH, MOE_GROUPS, MOE_EXPERTS, MOE_D_FF, D_MODEL), MOE_D_FF ** -0.5),
    }

def reference(x, mix_norm, ffn_norm, ab_w_in, a_q_norm, a_k_norm, b_q_norm, b_k_norm, b_sink, ab_w_out,
              c_w_in, c_q_norm, c_k_norm, c_w_out, moe_group_w, moe_group_b, moe_expert_w, moe_expert_b,
              moe_w_gate, moe_w_up, moe_w_down):
    for layer in range(DEPTH):
        i = layer // 2
        h = _rmsnorm(x, mix_norm[layer])
        if layer % 2 == 0:
            x = x + _mixer_ab(h, ab_w_in[i], a_q_norm[i], a_k_norm[i], b_q_norm[i], b_k_norm[i],
                              b_sink[i], ab_w_out[i])
        else:
            x = x + _mixer_c(h, c_w_in[i], c_q_norm[i], c_k_norm[i], c_w_out[i])
        h = _rmsnorm(x, ffn_norm[layer])
        x = x + _hier_moe(h, moe_group_w[layer], moe_group_b[layer], moe_expert_w[layer], moe_expert_b[layer],
                          moe_w_gate[layer], moe_w_up[layer], moe_w_down[layer])
    return x


_drawn_inputs = setup_inputs


def setup_inputs(seed=0):
    import zlib

    import numpy as np

    out = dict(_drawn_inputs(seed))
    spreads = {}
    factors = {'a_q_norm': 4.461,
     'a_k_norm': 4.843,
     'b_q_norm': 4.103,
     'b_k_norm': 5.337,
     'c_q_norm': 6.049,
     'c_k_norm': 5.5,
     'moe_group_b': 4.681}
    for name, (base, spread) in spreads.items():
        noise = np.random.default_rng([zlib.crc32(name.encode()), seed]).standard_normal(out[name].shape)
        drawn = base * np.exp(spread * noise) if base else spread * noise
        out[name] = jnp.asarray(drawn.astype(out[name].dtype))
    for name, factor in factors.items():
        out[name] = (out[name] * factor).astype(out[name].dtype)
    return out
```

```python
from contextlib import ExitStack

import numpy as np
import concourse.bass as bass
from concourse import mybir

ALU = mybir.AluOpType
ACT = mybir.ActivationFunctionType
F32 = mybir.dt.float32
I32 = mybir.dt.int32
AX = mybir.AxisListType.X

P = 128
D = 1024
SEQ = 256
NT = SEQ // P
NC = D // P
HD = 64
HEADS = 16
A_HEADS = B_HEADS = 8
GRID_W = 64
EPS = 1e-6
GROUPS, PER_GROUP = 4, 8
EXPERTS = GROUPS * PER_GROUP
DFF = 256
NR = GROUPS + EXPERTS
PAIRS = 2 * SEQ
NARROW, WIDE = 64, 256
SORTED = PAIRS + WIDE
HALF = 512
FAR = 1e30
UNIT = 2048
RING = 12
TURN = RING // 3
SLABS = (9, 6)
OUTS = 4

C_IDENT = 0
C_TRI = C_IDENT + P
C_ONES = C_TRI + P
C_IOTA = C_ONES + P
C_DIST = C_IOTA + PAIRS
C_MA = C_DIST + NT * SEQ
C_MB = C_MA + NT * SEQ
C_COS = C_MB + NT * SEQ
C_SIN = C_COS + NT * HD
C_REV4 = C_SIN + NT * HD
C_REV32 = C_REV4 + GROUPS
C_TRIE = C_REV32 + EXPERTS
C_ALL = C_TRIE + EXPERTS


def shape_constants():
    t = np.zeros((P, C_ALL), np.float32)
    t[:, C_IDENT:C_IDENT + P] = np.eye(P)
    t[:, C_TRI:C_TRI + P] = np.triu(np.ones((P, P)), 1)
    t[:, C_ONES:C_ONES + P] = 1.0
    t[:, C_IOTA:C_IOTA + PAIRS] = np.arange(PAIRS)[None]
    q = (np.arange(NT)[None, :, None] * P + np.arange(P)[:, None, None])
    k = np.arange(SEQ)[None, None, :]
    dist = np.abs(q - k)
    t[:, C_DIST:C_DIST + NT * SEQ] = dist.reshape(P, -1)
    count = (dist <= 64).astype(int)
    for window, dil in ((512, 4), (2048, 16)):
        count = count + ((dist % dil == 0) & (dist <= window // 2))
    t[:, C_MA:C_MA + NT * SEQ] = np.where(count > 0, -np.log(np.maximum(count, 1)), FAR).reshape(P, -1)
    t[:, C_MB:C_MB + NT * SEQ] = np.where(dist <= 128, 0.0, FAR).reshape(P, -1)
    inv_freq = np.float32(10000.0) ** (-np.arange(0, 32, 2, dtype=np.float32) / np.float32(32))
    tok = q[:, :, 0]
    cos, sin = [], []
    for axis in ((tok // GRID_W), (tok % GRID_W)):
        ang = (axis.astype(np.float32)[..., None] * inv_freq).astype(np.float32)
        cos += [np.cos(ang), np.cos(ang)]
        sin += [-np.sin(ang), np.sin(ang)]
    t[:, C_COS:C_COS + NT * HD] = np.concatenate(cos, -1).reshape(P, -1)
    t[:, C_SIN:C_SIN + NT * HD] = np.concatenate(sin, -1).reshape(P, -1)
    t[:, C_REV4:C_REV4 + GROUPS] = np.arange(GROUPS, 0, -1)[None]
    t[:, C_REV32:C_REV32 + EXPERTS] = np.arange(EXPERTS, 0, -1)[None]
    t[:EXPERTS, C_TRIE:C_TRIE + EXPERTS] = np.triu(np.ones((EXPERTS, EXPERTS)), 1)
    return t


def slope(i):
    return float(np.float32(2.0 ** (-8.0 * (i + 1) / HEADS)))


def first_unit(layer, part):
    at = 0 if layer == 0 else SLABS[0] + OUTS + 3 * EXPERTS
    return at + {"in": 0, "out": SLABS[layer], "experts": SLABS[layer] + OUTS}[part]


def hybrid_moe_kernel(nc, x_d, mix_norm, ffn_norm, ab_w_in, a_q_norm, a_k_norm, b_q_norm, b_k_norm, b_sink,
                      ab_w_out, c_w_in, c_q_norm, c_k_norm, c_w_out, moe_group_w, moe_group_b, moe_expert_w,
                      moe_expert_b, moe_w_gate, moe_w_up, moe_w_down, cst_d, out_d):
    with ExitStack() as ctx:
        def sb(name, shape, dt=F32):
            return ctx.enter_context(nc.sbuf_tensor(name, shape, dt))

        def sem(name):
            return ctx.enter_context(nc.semaphore(name))

        ring = [sb(f"ring{i}", [P, UNIT]) for i in range(RING)]
        x = sb("x", [P, NT, D])
        hsort = sb("hsort", [P, NC, SORTED])
        osort = sb("osort", [P, NC, SORTED])
        cst = sb("cst", [P, C_ALL])
        pairs_wT = sb("pairs_wT", [P, 4, SEQ])
        prob = sb("prob", [P, 2, NT, SEQ])
        square = sb("square", [P, 2, HALF])
        normed = sb("normed", [P, 2, HALF])
        rot = sb("rot", [P, 2, HALF])
        silu = sb("silu", [P, 2, WIDE])
        hidden = sb("hidden", [P, 2, WIDE])
        router_w = sb("router_w", [P, 2, NC, NR])
        router_gw = sb("router_gw", [P, 2, NC * GROUPS])
        router_ew = sb("router_ew", [P, 2, GROUPS, NC * PER_GROUP])
        router_b = sb("router_b", [P, 2, NR])
        gains = sb("gains", [P, 4, NC])
        head_g = sb("head_g", [P, 4])
        gq_bc = sb("gq_bc", [P, HD])
        gk_bc = sb("gk_bc", [P, HD])
        rope = sb("rope", [P, 4, NT, HD])
        sink = sb("sink", [P, B_HEADS])
        neg_sink = sb("neg_sink", [P, B_HEADS])
        sumsq = sb("sumsq", [P, NT])
        mean = sb("mean", [P, NT])
        rstd = sb("rstd", [P, NT])
        newton = sb("newton", [P, 2, NT * 4])
        head_ss = sb("head_ss", [P, NT * 4])
        head_rs = sb("head_rs", [P, NT * 4])
        negmax = sb("negmax", [P, 4, NT, 4])
        rowsum = sb("rowsum", [P, 4, NT, 4])
        rowinv = sb("rowinv", [P, NT, 4])
        sink_e = sb("sink_e", [P, NT, 4])
        logit = sb("logit", [P, NT, NR])
        r_g = sb("r_g", [P, 6, NT, GROUPS])
        r_e = sb("r_e", [P, 8, NT, EXPERTS])
        r_s = sb("r_s", [P, 20, NT])
        cnt_col = sb("cnt_col", [EXPERTS, P])
        starts = sb("starts", [1, EXPERTS + 1], I32)
        cntmax = sb("cntmax", [1, 1])
        banks = ctx.enter_context(nc.psum_tensor("banks", [P, 8, HALF], F32))

        hflat = hsort[:, :, :].rearrange("p a b -> p (a b)")
        oflat = osort[:, :, :].rearrange("p a b -> p (a b)")
        HT_TILES = 14
        headsT = hflat[:, 0:HT_TILES * SEQ].rearrange("p (n t) -> p n t", t=SEQ)
        VW = 640
        values = hflat[:, HT_TILES * SEQ:HT_TILES * SEQ + NT * VW].rearrange("p (t n) -> p t n", t=NT)
        tb0 = HT_TILES * SEQ + NT * VW
        bias = hflat[:, tb0:tb0 + 2 * HALF].rearrange("p (b t k) -> p b t k", b=2, t=NT)
        rows_out = hflat[:, 0:4 * D].rearrange("p (s d) -> p s d", s=4)
        tokens = oflat[:, 0:2048].rearrange("p (t c k) -> p t c k", t=NT, c=NC)
        att = oflat[:, 0:2048].rearrange("p (t n) -> p t n", t=NT)
        tokT = oflat[:, 2048:4096].rearrange("p (c t) -> p c t", c=NC)
        attT = tokT
        pairs = oflat[:, 4096:5120].rearrange("p (t s) -> p t s", t=NT)
        pairs_w = oflat[:, 5120:6144].rearrange("p (t s) -> p t s", t=NT)
        score = oflat[:, 4096:5120].rearrange("p (b t k) -> p b t k", b=2, t=NT)
        probT = oflat[:, 5120:6144].rearrange("p (b c q) -> p b c q", b=2, c=NT)

        ident = cst[:, C_IDENT:C_IDENT + P]
        tri = cst[:, C_TRI:C_TRI + P]
        ones = cst[:, C_ONES:C_ONES + P]
        iota = cst[:, C_IOTA:C_IOTA + PAIRS]
        trie = cst[0:EXPERTS, C_TRIE:C_TRIE + EXPERTS]

        def bank(i):
            return banks[:, i, :]

        def bank2(i, a):
            return banks[:, i, :].rearrange("p (a b) -> p a b", a=a)

        gate_ps = bank2(0, 2)
        up_ps = bank2(1, 2)
        down_narrow = bank2(4, NC)
        down_wide = banks[:, 4:8, :].rearrange("p b (a w) -> p (b a) w", a=2)
        Y_MIX = [[6, 7], [0, 1]]
        Y_MOE = [[4, 5], [6, 7]]

        s_x = sem("x_loaded")
        s_first = sem("first_constants_loaded")
        s_small = sem("small_inputs_loaded")
        s_unit = [sem(f"unit_loaded{i}") for i in range(RING)]
        s_used = sem("units_used")
        s_prep = sem("pool_prepared")
        s_pchain = sem("pool_chain")
        s_bias = sem("bias_ready")
        s_tail = sem("tail_cleared")
        s_dve = sem("dve_chain")
        s_x0 = sem("x_updated")
        s_sq = sem("act_square_sum")
        s_tok = sem("tokens_normalised")
        s_tokT_ps = sem("tokT_in_psum")
        s_tokT_a = sem("tokT_by_act")
        s_tokT_v = sem("tokT_by_dve")
        s_sqh = sem("head_squares")
        s_slab = sem("slab_taken")
        s_val = sem("values_taken")
        s_hT_ps = sem("headT_in_psum")
        s_hT = sem("headT_ready")
        s_sc_ps = sem("scores_in_psum")
        s_sc = sem("scores_max_ready")
        s_p = sem("prob_ready")
        s_pT_ps = sem("probT_in_psum")
        s_pT = sem("probT_ready")
        s_pv = sem("pv_done")
        s_sinkv = sem("sink_exponent")
        s_sink = sem("sink_term")
        s_att = sem("att_rows_ready")
        s_aT_ps = sem("attT_in_psum")
        s_aT = sem("attT_ready")
        s_rl_ps = sem("router_logits")
        s_rd = sem("router_differences")
        s_re = sem("router_exponentials")
        s_pick = sem("experts_picked")
        s_cc_ps = sem("counts_in_psum")
        s_cc = sem("counts_taken")
        s_pos_ps = sem("positions_in_psum")
        s_starts = sem("starts_ready")
        s_pairs = sem("pairs_ready")
        s_g_ps = sem("gathered_in_psum")
        s_g_a = sem("gathered_by_act")
        s_g_v = sem("gathered_by_dve")
        s_pairsw = sem("weighted_pairs_ready")
        s_wT_ps = sem("weightedT_in_psum")
        s_wT = sem("weightedT_ready")
        s_silu = sem("silu_ready")
        s_hid = sem("hidden_ready")
        s_out = sem("expert_output_taken")
        s_ro_ps = sem("rows_in_psum")
        s_ro_a = sem("rows_by_act")
        s_ro_v = sem("rows_by_dve")
        s_y = sem("y_ready")
        s_done = sem("output_stored")

        def loaded(n):
            return 16 * (n // RING + 1)

        def over_experts(eng, body):
            with eng.Fori(0, EXPERTS // TURN) as turn:
                for place in range(TURN):
                    body(turn, place)

        def head_place(layer, h):
            if layer == 1:
                return h // 2, 8 + h // 4, HD * (h % 2), HD * (h // 4)
            if h < A_HEADS:
                return h // 2, 4 + h // 2, HD * (h % 2), HD * h
            return 8 + (h - 8) // 2, 12 + (h - 8) // 4, HD * (h % 2), 512 + HD * ((h - 8) // 4)

        SLAB_PLAN = [
            [("heads", 0, 0), ("heads", 2, 0), ("heads", 4, 1), ("heads", 6, 1), ("values", 0, None),
             ("values", 256, None), ("heads", 8, 2), ("heads", 10, 2), ("shared2", 12, 3)],
            [("heads", 0, "q"), ("heads", 2, "q"), ("heads", 4, "q"), ("heads", 6, "q"),
             ("shared4", 8, "k"), ("values", 0, None)],
        ]
        TURNS = [[], []]
        for lay in range(2):
            for s, (kind, tile, g) in enumerate(SLAB_PLAN[lay]):
                if kind in ("heads", "shared2"):
                    TURNS[lay].append((s, tile, g, 0))
                elif kind == "shared4":
                    TURNS[lay] += [(s, tile, g, 0), (s, tile + 2, g, 1)]

        def turns_before(layer, slab):
            return (len(TURNS[0]) if layer else 0) + sum(t[0] < slab for t in TURNS[layer])

        def norm_slabs_before(layer, slab):
            n = sum(k != "values" for k, _, _ in SLAB_PLAN[0]) if layer else 0
            return n + sum(k != "values" for k, _, _ in SLAB_PLAN[layer][:slab])

        NORMED = [(lay, s) for lay in range(2) for s in range(SLABS[lay]) if SLAB_PLAN[lay][s][0] != "values"]

        def values_before(layer, slab):
            n = sum(k in ("values", "shared2") for k, _, _ in SLAB_PLAN[0]) if layer else 0
            return n + sum(k in ("values", "shared2") for k, _, _ in SLAB_PLAN[layer][:slab])

        def head_rows(layer, s, k, part):
            if SLAB_PLAN[layer][s][0] == "shared4":
                return normed[:, part, :].rearrange("p (t n) -> p t n", t=NT)
            return normed[:, k, :].rearrange("p (t n) -> p t n", t=NT)

        block = ctx.enter_context(nc.Block())

        @block.sync
        def _(sp):
            for t in range(NT):
                sp.dma_start(x[:, t, :], x_d[0, t * P:(t + 1) * P, :]).then_inc(s_x, 16)

            def room(n):
                if isinstance(n, int) and n < RING:
                    return
                sp.wait_ge(s_used, n - RING + 1)

            for layer in range(2):
                w_in = (ab_w_in, c_w_in)[layer][0].rearrange("(p c) n -> p c n", c=NC)
                for s in range(SLABS[layer]):
                    n = first_unit(layer, "in") + s
                    room(n)
                    sp.dma_start(ring[n % RING][:, :].rearrange("p (c n) -> p c n", c=NC),
                                 w_in[:, :, 256 * s:256 * s + 256]).then_inc(s_unit[n % RING], 16)
                w_out = (ab_w_out, c_w_out)[layer][0]
                for s in range(OUTS):
                    n = first_unit(layer, "out") + s
                    room(n)
                    sp.dma_start(ring[n % RING][:, :].rearrange("p (c n) -> p c n", c=2),
                                 w_out[256 * s:256 * s + 256, :].rearrange("(c p) n -> p c n", p=P))\
                        .then_inc(s_unit[n % RING], 16)
                base = first_unit(layer, "experts")
                gate = moe_w_gate[layer].rearrange("g e (p c) f -> (g e) p (c f)", c=NC)
                up = moe_w_up[layer].rearrange("g e (p c) f -> (g e) p (c f)", c=NC)
                down = moe_w_down[layer].rearrange("g e (c p) n -> (g e) p c n", p=P)

                def load_expert(turn, place):
                    e = turn * TURN + place
                    for m, w in enumerate((gate, up, down)):
                        k = base + 3 * place + m
                        room(turn * RING + k)
                        if m < 2:
                            src, dst = w[bass.ds(e, 1), :, :].rearrange("e p f -> p (e f)"), ring[k % RING][:, :]
                        else:
                            src = w[bass.ds(e, 1), :, :, :].rearrange("e p c n -> p (e c) n")
                            dst = ring[k % RING][:, :].rearrange("p (c n) -> p c n", c=2)
                        sp.dma_start(dst, src).then_inc(s_unit[k % RING], 16)

                over_experts(sp, load_expert)
            for t in range(NT):
                sp.wait_ge(s_x0, 3 * NT + t + 1)
                sp.dma_start(out_d[0, t * P:(t + 1) * P, :], x[:, t, :]).then_inc(s_done, 16)
            sp.wait_ge(s_done, 16 * NT)

        SMALL = 22

        @block.gpsimd
        def _(pool):
            n = [0]

            def link(ins):
                n[0] += 1
                ins.then_inc(s_pchain, 1)
                pool.wait_ge(s_pchain, n[0])

            pool.wait_ge(s_first, 16)
            pool.wait_ge(s_small, 16 * SMALL)
            for c in (0, 2):
                link(nc.gpsimd.tensor_scalar(head_g[:, c:c + 1], head_g[:, c:c + 1], -1.0, None, ALU.mult))
            for c in (1, 3):
                link(nc.gpsimd.tensor_scalar(head_g[:, c:c + 1], head_g[:, c:c + 1], 8.0, None, ALU.mult))
            nc.gpsimd.tensor_scalar(neg_sink[:, :], sink[:, :], -1.0, None, ALU.mult).then_inc(s_prep, 1)

            def table(h):
                if h >= 2:
                    pool.wait_ge(s_sc, 2 * (h - 1))
                mask = (C_MA, C_MB)[h // A_HEADS]
                i = 2 * h if h < A_HEADS else 2 * (h - A_HEADS) + 1
                b = bias[:, h % 2, :, :].rearrange("p t k -> p (t k)")
                link(nc.gpsimd.tensor_scalar(b, cst[:, C_DIST:C_DIST + HALF], slope(i), None, ALU.mult))
                nc.gpsimd.tensor_tensor(b, b, cst[:, mask:mask + HALF], ALU.add).then_inc(s_bias, 1)

            for h in range(2):
                table(h)
            for layer in range(2):
                nc.gpsimd.tensor_copy(router_w[:, layer, :, 0:GROUPS],
                                      router_gw[:, layer, :].rearrange("p (c g) -> p c g", c=NC)).then_inc(s_prep, 1)
                for g in range(GROUPS):
                    a = GROUPS + g * PER_GROUP
                    nc.gpsimd.tensor_copy(router_w[:, layer, :, a:a + PER_GROUP],
                                          router_ew[:, layer, g, :].rearrange("p (c e) -> p c e", c=NC))\
                        .then_inc(s_prep, 1)
            for i, (g, scale) in enumerate(((gq_bc, -1.0), (gk_bc, 8.0))):
                link(nc.gpsimd.tensor_scalar(g[:, :], g[:, :], scale, None, ALU.mult))
                for t in range(NT):
                    nc.gpsimd.tensor_tensor(rope[:, 2 * i, t, :], cst[:, C_COS + HD * t:C_COS + HD * t + HD],
                                            g[:, :], ALU.mult).then_inc(s_prep, 1)
                    for b in range(2):
                        sin_v = cst[:, C_SIN + HD * t:C_SIN + HD * t + HD].rearrange("p (a b j) -> p a b j", a=2, b=2)
                        nc.gpsimd.tensor_tensor(
                            rope[:, 2 * i + 1, t, :].rearrange("p (a b j) -> p a b j", a=2, b=2)[:, :, b, :],
                            sin_v[:, :, b, :],
                            g[:, :].rearrange("p (a b j) -> p a b j", a=2, b=2)[:, :, 1 - b, :],
                            ALU.mult).then_inc(s_prep, 1)
            for h in range(2, HEADS):
                table(h)
            for layer in range(2):
                pool.wait_ge(s_tok, NT * (2 * layer + 2))
                nc.gpsimd.memset(hsort[:, :, PAIRS:SORTED], 0.0).then_inc(s_tail, 1)

        PREP = 1 + 2 * (1 + GROUPS) + 2 * NT * 3

        @block.tensor
        def _(pe):
            def transpose_tokens(m):
                if m == 0:
                    pe.wait_ge(s_first, 16)
                for pair in range(NC // 2):
                    for c in range(2):
                        for t in range(NT):
                            if pair == 0 and c == 0:
                                pe.wait_ge(s_tok, NT * m + t + 1)
                            a = (c * NT + t) * P
                            ins = pe.transpose(bank(2 + pair)[:, a:a + P], tokens[:, t, 2 * pair + c, :], ident)
                    ins.then_inc(s_tokT_ps, 1)

            def tokT_ready(m):
                pe.wait_ge(s_tokT_a, 4 * (m + 1))
                pe.wait_ge(s_tokT_v, 4 * (m + 1))

            def slab(layer, s):
                n = first_unit(layer, "in") + s
                g = s + SLABS[0] * layer
                if s >= 2:
                    pe.wait_ge(s_slab, norm_slabs_before(layer, s - 1))
                    pe.wait_ge(s_val, values_before(layer, s - 1))
                pe.wait_ge(s_unit[n % RING], loaded(n))
                w = ring[n % RING][:, :].rearrange("p (c n) -> p c n", c=NC)
                for t in range(NT):
                    for c in range(NC):
                        ins = pe.matmul(bank2(s % 2, NT)[:, t, :], tokT[:, c, t * P:(t + 1) * P], w[:, c, :],
                                        start=(c == 0), stop=(c == NC - 1))
                ins.then_inc(s_used, 1)

            def turn_heads(layer, s):
                done = turns_before(layer, s)
                for (ts, tile, g, part) in TURNS[layer]:
                    if ts != s:
                        continue
                    b = done % 2
                    pe.wait_ge(s_slab, norm_slabs_before(layer, s) + 1)
                    if done >= 2:
                        pe.wait_ge(s_hT, done - 1)
                    k = norm_slabs_before(layer, s) % 2
                    for c in range(2):
                        for t in range(NT):
                            src = head_rows(layer, s, k, part)[:, t, c * P:(c + 1) * P]
                            ins = pe.transpose(bank2(2 + b, 2)[:, c, t * P:(t + 1) * P], src, ident)
                    ins.then_inc(s_hT_ps, 1)
                    done += 1

            def scores(layer, h):
                g = HEADS * layer + h
                qt, kt, r, _ = head_place(layer, h)
                if h == 0:
                    pe.wait_ge(s_hT, turns_before(layer, SLABS[layer]))
                    pe.wait_ge(s_slab, norm_slabs_before(layer, SLABS[layer]))
                    pe.wait_ge(s_val, values_before(layer, SLABS[layer]))
                if h >= 2:
                    if layer == 0:
                        pe.wait_ge(s_sc, NT * (g - 1))
                    else:
                        pe.wait_ge(s_p, g - 1)
                for t in range(NT):
                    ins = pe.matmul(bank2(h % 2, NT)[:, t, :], headsT[r:r + HD, qt, t * P:(t + 1) * P],
                                    headsT[r:r + HD, kt, :], start=True, stop=True)
                ins.then_inc(s_sc_ps, 1)

            def turn_prob(layer, h):
                g = HEADS * layer + h
                pe.wait_ge(s_p, g + 1)
                if h >= 2:
                    pe.wait_ge(s_pT, g - 1)
                for c in range(NT):
                    for t in range(NT):
                        ins = pe.transpose(bank2(2 + h % 2, NT)[:, c, t * P:(t + 1) * P],
                                           prob[:, h % 2, t, c * P:(c + 1) * P], ident)
                ins.then_inc(s_pT_ps, 1)

            def prob_values(layer, h):
                g = HEADS * layer + h
                u, j = h // 4, h % 4
                vcol = head_place(layer, h)[3]
                pe.wait_ge(s_pT, g + 1)
                if j == 0 and u >= 2:
                    pe.wait_ge(s_aT, 4 * layer + u - 1)
                o = bank2(4 + u % 2, NT)
                for t in range(NT):
                    for c in range(NT):
                        ins = pe.matmul(o[:, t, j * HD:(j + 1) * HD], probT[:, h % 2, c, t * P:(t + 1) * P],
                                        values[:, c, vcol:vcol + HD], start=(c == 0), stop=(c == NT - 1))
                ins.then_inc(s_pv, 1)

            def turn_att(layer, u):
                pe.wait_ge(s_att, 4 * layer + u + 1)
                b = 4 + u % 2
                for c in range(2):
                    for t in range(NT):
                        a = 256 * u + c * P
                        ins = pe.transpose(bank2(b, 2)[:, c, t * P:(t + 1) * P], att[:, t, a:a + P], ident)
                ins.then_inc(s_aT_ps, 1)

            def project_out(layer, u):
                n = first_unit(layer, "out") + u
                pe.wait_ge(s_aT, 4 * layer + u + 1)
                pe.wait_ge(s_unit[n % RING], loaded(n))
                w = ring[n % RING][:, :].rearrange("p (c n) -> p c n", c=2)
                for t in range(NT):
                    for half in range(2):
                        for c in range(2):
                            k = 2 * u + c
                            ins = pe.matmul(bank(Y_MIX[t][half]), attT[:, k, t * P:(t + 1) * P],
                                            w[:, c, half * HALF:(half + 1) * HALF],
                                            start=(k == 0), stop=(k == NC - 1))
                ins.then_inc(s_used, 1)

            def router(layer):
                if layer == 0:
                    pe.wait_ge(s_prep, PREP)
                for t in range(NT):
                    for c in range(NC):
                        ins = pe.matmul(bank(6)[:, t * NR:(t + 1) * NR], tokT[:, c, t * P:(t + 1) * P],
                                        router_w[:, layer, c, :], start=(c == 0), stop=(c == NC - 1))
                ins.then_inc(s_rl_ps, 1)
                pe.wait_ge(s_pick, layer + 1)
                picked = r_e[:, 7, :, :]
                for t in range(NT):
                    ins = pe.matmul(bank(7)[0:EXPERTS, 0:P], picked[:, t, :], ones, start=(t == 0), stop=(t == NT - 1))
                ins.then_inc(s_cc_ps, 1)
                for t in range(NT):
                    pe.matmul(bank(1)[:, 0:EXPERTS], ones, picked[:, t, :], start=(t == 0), stop=(t == NT - 1))
                pe.wait_ge(s_cc, layer + 1)
                pe.matmul(bank(1)[:, EXPERTS:2 * EXPERTS], cnt_col[:, :], trie, start=True, stop=True)
                for t in range(NT):
                    o = bank(0)[:, t * EXPERTS:(t + 1) * EXPERTS]
                    pe.matmul(o, cnt_col[:, :], trie, start=True, stop=False)
                    for b in range(t):
                        pe.matmul(o, ones, picked[:, b, :], start=False, stop=False)
                    ins = pe.matmul(o, tri, picked[:, t, :], start=False, stop=True)
                ins.then_inc(s_pos_ps, 1)

            def gather(layer):
                pe.wait_ge(s_pairs, layer + 1)
                for c in range(NC):
                    if c >= 4:
                        pe.wait_ge((s_g_a, s_g_v)[c % 2], 4 * layer + (c - 4) // 2 + 1)
                    for t in range(NT):
                        ins = pe.matmul(bank(2 + c % 4), tokens[:, t, c, :], pairs[:, t, :],
                                        start=(t == 0), stop=(t == NT - 1))
                    ins.then_inc(s_g_ps, 1)
                pe.wait_ge(s_pairsw, layer + 1)
                for b in range(2):
                    for s in range(2):
                        for t in range(NT):
                            a = (2 * b + s) * P
                            ins = pe.transpose(bank2(6 + b, 2)[:, s, t * P:(t + 1) * P], pairs_w[:, t, a:a + P], ident)
                    ins.then_inc(s_wT_ps, 1)

            def experts(layer, width, narrow):
                base = first_unit(layer, "experts")
                down_ps = down_narrow if narrow else down_wide

                def expert(turn, place):
                    e = turn * TURN + place
                    start = pe.value_load(starts[0:1, bass.ds(e, 1)], min_val=0, max_val=PAIRS)
                    for m, ps in enumerate((gate_ps, up_ps)):
                        k = base + 3 * place + m
                        pe.wait_ge(s_unit[k % RING], 16 * turn + loaded(k))
                        w = ring[k % RING][:, :].rearrange("p (c n) -> p c n", c=NC)
                        for f in range(2):
                            for c in range(NC):
                                ins = pe.matmul(ps[:, f, 0:width], w[:, c, f * P:(f + 1) * P],
                                                hsort[:, c, bass.ds(start, width)],
                                                start=(c == 0), stop=(c == NC - 1))
                        ins.then_inc(s_used, 1)
                    k = base + 3 * place + 2
                    pe.wait_ge(s_unit[k % RING], 16 * turn + loaded(k))
                    pe.wait_ge(s_out, EXPERTS * layer + e)
                    pe.wait_ge(s_hid, EXPERTS * layer + e + 1)
                    w = ring[k % RING][:, :].rearrange("p (c n) -> p c n", c=2)
                    for n in range(NC):
                        for c in range(2):
                            ins = pe.matmul(down_ps[:, n, 0:width], w[:, c, n * P:(n + 1) * P],
                                            hidden[:, c, 0:width], start=(c == 0), stop=(c == 1))
                    ins.then_inc(s_used, 1)

                over_experts(pe, expert)

            def combine(layer):
                pe.wait_ge(s_out, EXPERTS * (layer + 1))
                for s in range(4):
                    for half in range(2):
                        i = 2 * s + half
                        if i >= 4:
                            pe.wait_ge((s_ro_a, s_ro_v)[i % 2], 4 * layer + (i - 4) // 2 + 1)
                        for j in range(4):
                            ins = pe.transpose(bank(i % 4)[:, j * P:(j + 1) * P],
                                               osort[:, 4 * half + j, s * P:(s + 1) * P], ident)
                        ins.then_inc(s_ro_ps, 1)
                pe.wait_ge(s_ro_a, 4 * (layer + 1))
                pe.wait_ge(s_ro_v, 4 * (layer + 1))
                for t in range(NT):
                    for half in range(2):
                        for s in range(4):
                            ins = pe.matmul(bank(Y_MOE[t][half]), pairs_wT[:, s, t * P:(t + 1) * P],
                                            rows_out[:, s, half * HALF:(half + 1) * HALF],
                                            start=(s == 0), stop=(s == 3))
                        ins.then_inc(s_y, 1)

            for layer in range(2):
                transpose_tokens(2 * layer)
                tokT_ready(2 * layer)
                for s in range(SLABS[layer] + 1):
                    if s < SLABS[layer]:
                        slab(layer, s)
                    if s >= 1:
                        turn_heads(layer, s - 1)
                for h in range(HEADS + 2):
                    if h < HEADS:
                        scores(layer, h)
                    if 1 <= h <= HEADS:
                        turn_prob(layer, h - 1)
                    if h >= 2:
                        prob_values(layer, h - 2)
                        if (h - 2) % 4 == 3:
                            turn_att(layer, (h - 2) // 4)
                for u in range(OUTS):
                    project_out(layer, u)
                transpose_tokens(2 * layer + 1)
                tokT_ready(2 * layer + 1)
                router(layer)
                gather(layer)
                pe.wait_ge(s_g_a, 4 * (layer + 1))
                pe.wait_ge(s_g_v, 4 * (layer + 1))
                pe.wait_ge(s_wT, 2 * (layer + 1))
                pe.wait_ge(s_tail, layer + 1)
                pe.wait_ge(s_starts, 2 * (layer + 1))
                most = pe.value_load(starts[0:1, EXPERTS:EXPERTS + 1], min_val=0, max_val=SEQ)
                with pe.If(most <= NARROW):
                    experts(layer, NARROW, True)
                with pe.Else():
                    experts(layer, WIDE, False)
                combine(layer)

        @block.scalar
        def _(act):
            act.dma_start(cst[:, :], cst_d).then_inc(s_first, 16)
            for m in range(2):
                for l in range(2):
                    act.dma_start(gains[:, 2 * l + m, :], (mix_norm, ffn_norm)[m][l].rearrange("(p c) -> p c", c=NC))\
                        .then_inc(s_small, 16)
            act.dma_start(gq_bc[:, :], c_q_norm[0].partition_broadcast(P)).then_inc(s_small, 16)
            count = 5
            for c, g in enumerate((a_q_norm, a_k_norm, b_q_norm, b_k_norm)):
                for r in range(2):
                    act.dma_start(head_g[r * HD:(r + 1) * HD, c:c + 1], g[0].rearrange("(p c) -> p c", c=1))\
                        .then_inc(s_small, 16)
                    count += 1
            act.dma_start(gk_bc[:, :], c_k_norm[0].partition_broadcast(P)).then_inc(s_small, 16)
            act.dma_start(sink[:, :], b_sink[0].partition_broadcast(P)).then_inc(s_small, 16)
            act.dma_start(router_gw[:, :, :], moe_group_w.rearrange("l (p c) g -> p l (c g)", c=NC)).then_inc(s_small, 16)
            count += 3
            for l in range(2):
                act.dma_start(router_ew[:, l, :, :], moe_expert_w[l].rearrange("g (p c) e -> p g (c e)", c=NC))\
                    .then_inc(s_small, 16)
                act.dma_start(router_b[:, l, 0:GROUPS], moe_group_b[l].partition_broadcast(P)).then_inc(s_small, 16)
                act.dma_start(router_b[:, l, GROUPS:NR],
                              moe_expert_b[l].rearrange("g e -> (g e)").partition_broadcast(P)).then_inc(s_small, 16)
                count += 3
            assert count == SMALL

            def square_sum(m):
                if m == 0:
                    act.wait_ge(s_x, 32)
                else:
                    act.wait_ge(s_x0, NT * (m - 1) + 1)
                nc.scalar.activation(square[:, :, :].rearrange("p a b -> p (a b)"), x[:, 0, :], ACT.Square,
                                     accum_out=sumsq[:, 0:1]).then_inc(s_sq, 1)

            def take_tokT(m):
                if m == 0:
                    act.wait_ge(s_small, 16 * SMALL)
                for pair in (0, 2):
                    act.wait_ge(s_tokT_ps, 4 * m + pair + 1)
                    for c in range(2):
                        k = 2 * pair + c
                        nc.scalar.activation(tokT[:, k, :], bank2(2 + pair, 2)[:, c, :], ACT.Copy,
                                             scale=gains[:, m, k:k + 1]).then_inc(s_tokT_a, 1)

            def slab(layer, s):
                kind, col, _ = SLAB_PLAN[layer][s]
                act.wait_ge(s_used, first_unit(layer, "in") + s + 1)
                ps = bank2(s % 2, NT)
                if kind == "values":
                    nc.scalar.activation(values[:, :, col:col + 256], ps, ACT.Copy).then_inc(s_val, 1)
                    return
                i = norm_slabs_before(layer, s)
                w = 2 * HD if kind == "shared2" else 4 * HD
                if kind == "shared2":
                    nc.scalar.activation(values[:, :, 512:640], ps[:, :, w:2 * w], ACT.Copy).then_inc(s_val, 1)
                if i >= 2:
                    act.wait_ge(s_slab, i - 1)
                nc.scalar.activation(square[:, i % 2, 0:NT * w].rearrange("p (t n) -> p t n", t=NT), ps[:, :, 0:w],
                                     ACT.Square).then_inc(s_sqh, 1)

            def take_heads(layer, s):
                i = turns_before(layer, s)
                for (ts, tile, g, part) in TURNS[layer]:
                    if ts != s:
                        continue
                    act.wait_ge(s_hT_ps, i + 1)
                    if i == 0:
                        act.wait_ge(s_prep, PREP)
                    scale = 1.0 if layer else head_g[:, g:g + 1]
                    nc.scalar.activation(headsT[:, tile:tile + 2, :], bank2(2 + i % 2, 2), ACT.Copy,
                                         scale=scale).then_inc(s_hT, 1)
                    i += 1

            def exponentials(layer, h):
                g = HEADS * layer + h
                act.wait_ge(s_sc, NT * (g + 1))
                if h >= 2:
                    act.wait_ge(s_pT_ps, g - 1)
                for t in range(NT):
                    src = score[:, h % 2, t, :] if layer == 0 else bank2(h % 2, NT)[:, t, :]
                    ins = nc.scalar.activation(prob[:, h % 2, t, :], src, ACT.Exp, scale=-1.0,
                                               bias=negmax[:, h // 4, t, h % 4:h % 4 + 1],
                                               accum_out=rowsum[:, h // 4, t, h % 4:h % 4 + 1])
                ins.then_inc(s_p, 1)

            def take_probT(layer, h):
                g = HEADS * layer + h
                act.wait_ge(s_pT_ps, g + 1)
                if h >= 2:
                    act.wait_ge(s_pv, g - 1)
                nc.scalar.activation(probT[:, h % 2, :, :], bank2(2 + h % 2, NT), ACT.Copy).then_inc(s_pT, 1)

            def take_attT(layer, u):
                act.wait_ge(s_aT_ps, 4 * layer + u + 1)
                nc.scalar.activation(attT[:, 2 * u:2 * u + 2, :], bank2(4 + u % 2, 2), ACT.Copy).then_inc(s_aT, 1)

            def sink_exp(u):
                act.wait_ge(s_sinkv, u - 1)
                nc.scalar.activation(sink_e[:, :, :], sink_e[:, :, :], ACT.Exp).then_inc(s_sink, 1)

            def router(layer):
                act.wait_ge(s_rd, 2 * layer + 1)
                nc.scalar.activation(r_g[:, 5, :, :], r_g[:, 4, :, :], ACT.Exp).then_inc(s_re, 1)
                act.wait_ge(s_rd, 2 * layer + 2)
                nc.scalar.activation(r_s[:, 6, :], r_s[:, 5, :], ACT.Exp).then_inc(s_re, 1)

            def gather(layer):
                for i in range(4):
                    c = 2 * i
                    act.wait_ge(s_g_ps, NC * layer + c + 1)
                    nc.scalar.activation(hsort[:, c, 0:PAIRS], bank(2 + c % 4), ACT.Copy,
                                         scale=gains[:, 2 * layer + 1, c:c + 1]).then_inc(s_g_a, 1)
                for b in range(2):
                    act.wait_ge(s_wT_ps, 2 * layer + b + 1)
                    nc.scalar.activation(pairs_wT[:, 2 * b:2 * b + 2, :], bank2(6 + b, 2), ACT.Copy).then_inc(s_wT, 1)

            def experts(layer, width):
                base = first_unit(layer, "experts")

                def expert(turn, place):
                    e = turn * TURN + place
                    act.wait_ge(s_used, base + 3 * place + 1 + turn * RING)
                    act.wait_ge(s_hid, EXPERTS * layer + e)
                    nc.scalar.activation(silu[:, :, 0:width], gate_ps[:, :, 0:width], ACT.Silu).then_inc(s_silu, 1)

                over_experts(act, expert)

            def rows(layer):
                for i in range(0, 8, 2):
                    act.wait_ge(s_ro_ps, 8 * layer + i + 1)
                    nc.scalar.activation(rows_out[:, i // 2, 0:HALF], bank(i % 4), ACT.Copy).then_inc(s_ro_a, 1)

            for layer in range(2):
                square_sum(2 * layer)
                take_tokT(2 * layer)
                for s in range(SLABS[layer] + 1):
                    if s < SLABS[layer]:
                        slab(layer, s)
                    if s >= 1:
                        take_heads(layer, s - 1)
                for h in range(HEADS + 2):
                    if h < HEADS:
                        exponentials(layer, h)
                    if 1 <= h <= HEADS and layer == 0:
                        take_probT(layer, h - 1)
                    if h >= 2 and (h - 2) % 4 == 3:
                        u = (h - 2) // 4
                        if layer == 0 and u >= 2:
                            sink_exp(u)
                        take_attT(layer, u)
                square_sum(2 * layer + 1)
                take_tokT(2 * layer + 1)
                router(layer)
                gather(layer)
                act.wait_ge(s_starts, 2 * (layer + 1))
                most = act.value_load(starts[0:1, EXPERTS:EXPERTS + 1], min_val=0, max_val=SEQ)
                with act.If(most <= NARROW):
                    experts(layer, NARROW)
                with act.Else():
                    experts(layer, WIDE)
                rows(layer)

        @block.vector
        def _(dve):
            n = [0]
            V = nc.vector

            def link(ins):
                n[0] += 1
                ins.then_inc(s_dve, 1)
                dve.wait_ge(s_dve, n[0])

            def inverse_root(y, v, k):
                half, cube = newton[:, 0, 0:k], newton[:, 1, 0:k]
                link(V.tensor_scalar(half.bitcast(I32), v.bitcast(I32), 1, None, ALU.logical_shift_right))
                link(V.tensor_scalar(y.bitcast(I32), half.bitcast(I32), -1.0, float(0x5f3759df), ALU.mult, ALU.add))
                for _ in range(3):
                    link(V.tensor_tensor(half, y, y, ALU.mult))
                    link(V.scalar_tensor_tensor(cube, half, -0.5, v, ALU.mult, ALU.mult))
                    link(V.scalar_tensor_tensor(y, cube, 1.5, y, ALU.add, ALU.mult))

            def normalise(m):
                if m == 0:
                    dve.wait_ge(s_x, 32)
                else:
                    dve.wait_ge(s_x0, NT * m)
                link(V.tensor_tensor_reduce(normed[:, :, :].rearrange("p a b -> p (a b)"), x[:, 1, :], x[:, 1, :],
                                            1.0, 0.0, ALU.mult, ALU.add, sumsq[:, 1:2]))
                dve.wait_ge(s_sq, m + 1)
                link(V.tensor_scalar(mean[:, :], sumsq[:, :], 1.0 / D, EPS, ALU.mult, ALU.add))
                inverse_root(rstd[:, :], mean[:, :], NT)
                for t in range(NT):
                    V.tensor_scalar(tokens[:, t, :, :], x[:, t, :].rearrange("q (p c) -> q c p", c=NC),
                                    rstd[:, t:t + 1], None, ALU.mult).then_inc(s_tok, 1)

            def take_tokT(m):
                if m == 0:
                    dve.wait_ge(s_small, 16 * SMALL)
                for pair in (1, 3):
                    dve.wait_ge(s_tokT_ps, 4 * m + pair + 1)
                    for c in range(2):
                        k = 2 * pair + c
                        V.tensor_scalar(tokT[:, k, :], bank2(2 + pair, 2)[:, c, :], gains[:, m, k:k + 1], None,
                                        ALU.mult).then_inc(s_tokT_v, 1)

            def slab(layer, s):
                kind, tile, g = SLAB_PLAN[layer][s]
                if kind == "values":
                    return
                i = norm_slabs_before(layer, s)
                nh = 2 if kind == "shared2" else 4
                w = nh * HD
                ps = bank2(s % 2, NT)[:, :, 0:w].rearrange("p t (h d) -> p t h d", d=HD)
                dve.wait_ge(s_sqh, i + 1)
                link(V.tensor_reduce(head_ss[:, 0:NT * nh],
                                     square[:, i % 2, 0:NT * w].rearrange("p (n d) -> p n d", d=HD), AX, ALU.add))
                link(V.tensor_scalar(head_ss[:, 0:NT * nh], head_ss[:, 0:NT * nh], HD * EPS, None, ALU.add))
                inverse_root(head_rs[:, 0:NT * nh], head_ss[:, 0:NT * nh], NT * nh)
                rs = head_rs[:, 0:NT * nh].rearrange("p (t h) -> p t h", t=NT).unsqueeze(3)\
                    .to_broadcast([P, NT, nh, HD])
                if i >= 2:
                    dve.wait_ge(s_hT_ps, turns_before(*NORMED[i - (kind != "shared4")]))
                if layer == 0:
                    dst = normed[:, i % 2, :].rearrange("p (t h d) -> p t h d", t=NT, d=HD)
                    if kind == "heads":
                        V.tensor_tensor(dst, ps, rs, ALU.mult).then_inc(s_slab, 1)
                    else:
                        dup = normed[:, i % 2, :].rearrange("p (t h r d) -> p t h r d", t=NT, r=2, d=HD)
                        link(V.tensor_tensor(dup[:, :, :, 0, :], ps, rs, ALU.mult))
                        V.tensor_tensor(dup[:, :, :, 1, :], ps, rs, ALU.mult).then_inc(s_slab, 1)
                    return
                flat = square[:, i % 2, :]
                link(V.tensor_tensor(flat.rearrange("p (t h d) -> p t h d", t=NT, d=HD), ps, rs, ALU.mult))
                tab = 0 if g == "q" else 2

                def swap(v, b):
                    return v.rearrange("p (h a b j) -> p (h a) b j", a=2, b=2, j=16)[:, :, b, :]

                for t in range(NT):
                    q = flat[:, t * w:(t + 1) * w]
                    r0 = rot[:, 0, t * w:(t + 1) * w]
                    r1 = rot[:, 1, t * w:(t + 1) * w]
                    cosb = rope[:, tab, t, :].unsqueeze(1).to_broadcast([P, 4, HD])
                    V.tensor_tensor(r0.rearrange("p (h d) -> p h d", d=HD), q.rearrange("p (h d) -> p h d", d=HD),
                                    cosb, ALU.mult).then_inc(s_dve, 1)
                    n[0] += 1
                    for b in range(2):
                        for a in range(2):
                            sinb = rope[:, tab + 1, t, 32 * a + 16 * b:32 * a + 16 * b + 16].unsqueeze(1)\
                                .to_broadcast([P, 4, 16])
                            V.tensor_tensor(
                                r1.rearrange("p (h d) -> p h d", d=HD)[:, :, 32 * a + 16 * b:32 * a + 16 * b + 16],
                                q.rearrange("p (h d) -> p h d", d=HD)[:, :, 32 * a + 16 * (1 - b):
                                                                     32 * a + 16 * (1 - b) + 16],
                                sinb, ALU.mult).then_inc(s_dve, 1)
                            n[0] += 1
                dve.wait_ge(s_dve, n[0])
                if kind == "heads":
                    V.tensor_tensor(normed[:, i % 2, :], rot[:, 0, :], rot[:, 1, :], ALU.add).then_inc(s_slab, 1)
                else:
                    for part in range(2):
                        dst = normed[:, part, :].rearrange("p (t h r d) -> p t h r d", t=NT, r=2, d=HD)
                        for r in range(2):
                            a = [rot[:, k, :].rearrange("p (t n) -> p t n", t=NT)[:, :, part * 2 * HD:(part + 1) * 2 * HD]
                                 .rearrange("p t (h d) -> p t h d", d=HD) for k in range(2)]
                            ins = V.tensor_tensor(dst[:, :, :, r, :], a[0], a[1], ALU.add)
                            if part == 0 or r == 0:
                                link(ins)
                    ins.then_inc(s_slab, 1)

            def maxima(layer, h):
                g = HEADS * layer + h
                u, j = h // 4, h % 4
                dve.wait_ge(s_sc_ps, g + 1)
                if layer == 0:
                    dve.wait_ge(s_bias, h + 1)
                    if h >= 2:
                        dve.wait_ge(s_p, h - 1)
                    for t in range(NT):
                        ins = V.tensor_tensor_reduce(score[:, h % 2, t, :], bank2(h % 2, NT)[:, t, :],
                                                     bias[:, h % 2, t, :], 1.0, 3.0e38, ALU.add, ALU.min,
                                                     negmax[:, u, t, j:j + 1])
                        if h < A_HEADS:
                            ins.then_inc(s_sc, 1)
                        else:
                            link(ins)
                    if h >= A_HEADS:
                        k = h - A_HEADS
                        V.tensor_tensor(negmax[:, u, :, j], negmax[:, u, :, j],
                                        neg_sink[:, k:k + 1].to_broadcast([P, NT]), ALU.min).then_inc(s_sc, NT)
                else:
                    V.tensor_reduce(negmax[:, u, :, j], bank2(h % 2, NT), AX, ALU.min).then_inc(s_sc, NT)

            def take_probT(layer, h):
                g = HEADS * layer + h
                dve.wait_ge(s_pT_ps, g + 1)
                if h >= 2:
                    dve.wait_ge(s_pv, g - 1)
                V.tensor_copy(probT[:, h % 2, :, :], bank2(2 + h % 2, NT)).then_inc(s_pT, 1)

            def att_rows(layer, u):
                dve.wait_ge(s_pv, HEADS * layer + 4 * u + 4)
                if layer == 0 and u >= 2:
                    k = 4 * (u - 2)
                    if u == 3:
                        dve.wait_ge(s_sink, 1)
                    V.tensor_tensor(sink_e[:, :, :], negmax[:, u, :, :],
                                    sink[:, k:k + 4].unsqueeze(1).to_broadcast([P, NT, 4]), ALU.add).then_inc(s_sinkv, 1)
                    dve.wait_ge(s_sink, u - 1)
                    link(V.tensor_tensor(rowsum[:, u, :, :], rowsum[:, u, :, :], sink_e[:, :, :], ALU.add))
                link(V.reciprocal(rowinv[:, :, :], rowsum[:, u, :, :]))
                V.tensor_tensor(att[:, :, 256 * u:256 * u + 256].rearrange("p t (h d) -> p t h d", d=HD),
                                bank2(4 + u % 2, NT).rearrange("p t (h d) -> p t h d", d=HD),
                                rowinv[:, :, :].unsqueeze(3).to_broadcast([P, NT, 4, HD]), ALU.mult)\
                    .then_inc(s_att, 1)

            def residual(where, done, value):
                dve.wait_ge(done, value)
                for t in range(NT):
                    for half in range(2):
                        xs = x[:, t, half * HALF:(half + 1) * HALF]
                        ins = V.tensor_tensor(xs, bank(where[t][half]), xs, ALU.add)
                        if half == 0:
                            n[0] += 1
                            ins.then_inc(s_dve, 1)
                            dve.wait_ge(s_dve, n[0])
                    ins.then_inc(s_x0, 1)

            def router(layer):
                G = [r_g[:, i, :, :] for i in range(6)]
                E = [r_e[:, i, :, :] for i in range(8)]
                S = [r_s[:, i, :] for i in range(20)]
                rev4 = cst[:, C_REV4:C_REV4 + GROUPS].unsqueeze(1).to_broadcast([P, NT, GROUPS])
                rev32 = cst[:, C_REV32:C_REV32 + EXPERTS].unsqueeze(1).to_broadcast([P, NT, EXPERTS])

                def over(s, k):
                    return s.unsqueeze(2).to_broadcast([P, NT, k])

                dve.wait_ge(s_rl_ps, layer + 1)
                link(V.tensor_tensor(logit[:, :, :], bank(6)[:, 0:NT * NR].rearrange("p (t n) -> p t n", t=NT),
                                     router_b[:, layer, :].unsqueeze(1).to_broadcast([P, NT, NR]), ALU.add))
                lg, le = logit[:, :, 0:GROUPS], logit[:, :, GROUPS:NR]
                link(V.tensor_reduce(S[0], lg, AX, ALU.max))
                V.tensor_tensor(G[4], lg, over(S[0], GROUPS), ALU.subtract).then_inc(s_rd, 1)
                link(V.tensor_tensor(G[0], lg, over(S[0], GROUPS), ALU.is_equal))
                link(V.tensor_tensor(G[1], G[0], rev4, ALU.mult))
                link(V.tensor_reduce(S[1], G[1], AX, ALU.max))
                link(V.tensor_tensor(G[2], G[1], over(S[1], GROUPS), ALU.is_equal))
                link(V.tensor_scalar(G[3], G[2], -1.0, 1.0e37, ALU.add, ALU.mult))
                link(V.tensor_tensor(E[0].rearrange("p t (g e) -> p t g e", g=GROUPS),
                                     le.rearrange("p t (g e) -> p t g e", g=GROUPS),
                                     G[3].unsqueeze(3).to_broadcast([P, NT, GROUPS, PER_GROUP]), ALU.add))

                def best(src, top, onehot):
                    link(V.tensor_reduce(top, src, AX, ALU.max))
                    link(V.tensor_tensor(E[1], src, over(top, EXPERTS), ALU.is_equal))
                    link(V.tensor_tensor(E[2], E[1], rev32, ALU.mult))
                    link(V.tensor_reduce(S[2], E[2], AX, ALU.max))
                    link(V.tensor_tensor(onehot, E[2], over(S[2], EXPERTS), ALU.is_equal))

                best(E[0], S[3], E[3])
                link(V.scalar_tensor_tensor(E[4], E[3], -3.0e37, E[0], ALU.mult, ALU.add))
                best(E[4], S[4], E[5])
                V.tensor_tensor(r_e[:, 7, :, :], E[3], E[5], ALU.add).then_inc(s_pick, 1)
                V.tensor_tensor(S[5], S[4], S[3], ALU.subtract).then_inc(s_rd, 1)
                dve.wait_ge(s_cc_ps, layer + 1)
                V.tensor_copy(cnt_col[:, :], bank(7)[0:EXPERTS, 0:P]).then_inc(s_cc, 1)
                dve.wait_ge(s_re, 2 * layer + 2)
                link(V.tensor_reduce(S[7], G[5], AX, ALU.add))
                link(V.tensor_scalar(S[8], S[6], 1.0, None, ALU.add))
                link(V.tensor_tensor(S[9], S[8], S[7], ALU.mult))
                link(V.reciprocal(S[10], S[9]))
                link(V.tensor_tensor(S[11], S[10], S[6], ALU.mult))
                dve.wait_ge(s_pos_ps, layer + 1)
                pos = bank(0)[:, 0:NT * EXPERTS].rearrange("p (t e) -> p t e", t=NT)
                for i in range(2):
                    link(V.tensor_tensor(E[6], pos, E[3 + 2 * i], ALU.mult))
                    link(V.tensor_reduce(S[12 + i], E[6], AX, ALU.add))
                for t in range(NT):
                    link(V.tensor_scalar(pairs_w[:, t, :], iota, S[12][:, t:t + 1], None, ALU.is_equal))
                    ins = V.scalar_tensor_tensor(pairs[:, t, :], iota, S[13][:, t:t + 1], pairs_w[:, t, :],
                                                 ALU.is_equal, ALU.add)
                    if t == 0:
                        link(ins)
                ins.then_inc(s_pairs, 1)
                dve.wait_ge(s_pairs, layer + 1)
                V.tensor_copy(starts[:, 0:EXPERTS], bank(1)[0:1, EXPERTS:2 * EXPERTS]).then_inc(s_starts, 1)
                link(V.tensor_reduce(cntmax[:, :], bank(1)[0:1, 0:EXPERTS], AX, ALU.max))
                V.tensor_copy(starts[:, EXPERTS:EXPERTS + 1], cntmax[:, :]).then_inc(s_starts, 1)
                for t in range(NT):
                    link(V.tensor_scalar(normed[:, 0, :], iota, S[12][:, t:t + 1], S[10][:, t:t + 1],
                                         ALU.is_equal, ALU.mult))
                    link(V.tensor_scalar(normed[:, 1, :], iota, S[13][:, t:t + 1], S[11][:, t:t + 1],
                                         ALU.is_equal, ALU.mult))
                    ins = V.tensor_tensor(pairs_w[:, t, :], normed[:, 0, :], normed[:, 1, :], ALU.add)
                    if t == 0:
                        link(ins)
                ins.then_inc(s_pairsw, 1)

            def gather(layer):
                for i in range(4):
                    c = 2 * i + 1
                    dve.wait_ge(s_g_ps, NC * layer + c + 1)
                    V.tensor_scalar(hsort[:, c, 0:PAIRS], bank(2 + c % 4), gains[:, 2 * layer + 1, c:c + 1], None,
                                    ALU.mult).then_inc(s_g_v, 1)

            def experts(layer, width, narrow):
                base = first_unit(layer, "experts")

                def expert(turn, place):
                    e = turn * TURN + place
                    start = dve.value_load(starts[0:1, bass.ds(e, 1)], min_val=0, max_val=PAIRS)
                    dve.wait_ge(s_used, base + 3 * place + 2 + turn * RING)
                    dve.wait_ge(s_silu, EXPERTS * layer + e + 1)
                    V.tensor_tensor(hidden[:, :, 0:width], up_ps[:, :, 0:width], silu[:, :, 0:width],
                                    ALU.mult).then_inc(s_hid, 1)
                    dve.wait_ge(s_used, base + 3 * place + 3 + turn * RING)
                    dve.wait_ge(s_out, EXPERTS * layer + e)
                    if narrow:
                        V.tensor_copy(osort[:, :, bass.ds(start, width)], down_narrow).then_inc(s_out, 1)
                    else:
                        for b in range(4):
                            ins = V.tensor_copy(osort[:, 2 * b:2 * b + 2, bass.ds(start, width)],
                                                down_wide[:, 2 * b:2 * b + 2, :])
                        ins.then_inc(s_out, 1)

                over_experts(dve, expert)

            def rows(layer):
                for i in range(1, 8, 2):
                    dve.wait_ge(s_ro_ps, 8 * layer + i + 1)
                    V.tensor_copy(rows_out[:, i // 2, HALF:D], bank(i % 4)).then_inc(s_ro_v, 1)

            for layer in range(2):
                normalise(2 * layer)
                take_tokT(2 * layer)
                for s in range(SLABS[layer]):
                    slab(layer, s)
                for h in range(HEADS + 2):
                    if h < HEADS:
                        maxima(layer, h)
                    if 1 <= h <= HEADS and layer == 1:
                        take_probT(layer, h - 1)
                    if h >= 2 and (h - 2) % 4 == 3:
                        att_rows(layer, (h - 2) // 4)
                residual(Y_MIX, s_used, first_unit(layer, "experts"))
                normalise(2 * layer + 1)
                take_tokT(2 * layer + 1)
                router(layer)
                gather(layer)
                dve.wait_ge(s_starts, 2 * (layer + 1))
                most = dve.value_load(starts[0:1, EXPERTS:EXPERTS + 1], min_val=0, max_val=SEQ)
                with dve.If(most <= NARROW):
                    experts(layer, NARROW, True)
                with dve.Else():
                    experts(layer, WIDE, False)
                rows(layer)
                residual(Y_MOE, s_y, 4 * (layer + 1))


_INS = ['x', 'mix_norm', 'ffn_norm', 'ab_w_in', 'a_q_norm', 'a_k_norm', 'b_q_norm', 'b_k_norm', 'b_sink',
        'ab_w_out', 'c_w_in', 'c_q_norm', 'c_k_norm', 'c_w_out', 'moe_group_w', 'moe_group_b', 'moe_expert_w',
        'moe_expert_b', 'moe_w_gate', 'moe_w_up', 'moe_w_down']


def kernel(**inputs):
    import concourse.bacc as bacc
    from concourse.bass_utils import run_bass_kernel_spmd

    nc = bacc.Bacc("TRN2", target_bir_lowering=False, num_devices=1)
    arrays, args = {}, []
    for name in _INS + ["shape_constants"]:
        a = shape_constants() if name == "shape_constants" else np.ascontiguousarray(inputs[name])
        arrays[f"in_{name}"] = a
        args.append(nc.dram_tensor(f"in_{name}", a.shape, F32, kind="ExternalInput").ap())
    out = nc.dram_tensor("out_x", (1, SEQ, D), F32, kind="ExternalOutput").ap()
    hybrid_moe_kernel(nc, *args, out)
    r = run_bass_kernel_spmd(nc, [arrays], core_ids=[0])
    return r.results[0]["out_x"]
```

```python
from contextlib import ExitStack

import numpy as np
import concourse.bass as bass
from concourse import mybir

ALU = mybir.AluOpType
ACT = mybir.ActivationFunctionType
F32 = mybir.dt.float32
I32 = mybir.dt.int32
AX = mybir.AxisListType.X

P = 128
D = 1024
SEQ = 256
NT = SEQ // P
NC = D // P
HD = 64
HEADS = 16
A_HEADS = B_HEADS = 8
GRID_W = 64
EPS = 1e-6
GROUPS, PER_GROUP = 4, 8
EXPERTS = GROUPS * PER_GROUP
DFF = 256
NR = GROUPS + EXPERTS
SLOTS = 32
ROUNDS = SEQ // SLOTS
BATCH = 4
BATCHES = EXPERTS // BATCH
HALF = 512
FAR = 1e30
UNIT = 2048
RING = 16
STAGE = BATCH
PER_BATCH = 3 * STAGE
PER_ROUND = 3 * EXPERTS
LOOP = 4
SLABS = (9, 6)
OUTS = 4

C_IDENT = 0
C_TRI = C_IDENT + P
C_ONES = C_TRI + P
C_IOTA = C_ONES + P
C_REV4 = C_IOTA + P
C_REV32 = C_REV4 + GROUPS
C_BASE = C_REV32 + EXPERTS
C_DIST = C_BASE + EXPERTS
C_MA = C_DIST + NT * SEQ
C_MB = C_MA + NT * SEQ
C_KEEP = C_MB + NT * SEQ
C_COS = C_KEEP
C_SIN = C_COS + NT * HD
C_ALL = C_SIN + NT * HD


def shape_constants():
    t = np.zeros((P, C_ALL), np.float32)
    t[:, C_IDENT:C_IDENT + P] = np.eye(P)
    t[:, C_TRI:C_TRI + P] = np.triu(np.ones((P, P)), 1)
    t[:, C_ONES:C_ONES + P] = 1.0
    t[:, C_IOTA:C_IOTA + P] = np.arange(P)[None]
    q = (np.arange(NT)[None, :, None] * P + np.arange(P)[:, None, None])
    k = np.arange(SEQ)[None, None, :]
    dist = np.abs(q - k)
    t[:, C_DIST:C_DIST + NT * SEQ] = dist.reshape(P, -1)
    count = (dist <= 64).astype(int)
    for window, dil in ((512, 4), (2048, 16)):
        count = count + ((dist % dil == 0) & (dist <= window // 2))
    t[:, C_MA:C_MA + NT * SEQ] = np.where(count > 0, -np.log(np.maximum(count, 1)), FAR).reshape(P, -1)
    t[:, C_MB:C_MB + NT * SEQ] = np.where(dist <= 128, 0.0, FAR).reshape(P, -1)
    inv_freq = np.float32(10000.0) ** (-np.arange(0, 32, 2, dtype=np.float32) / np.float32(32))
    tok = q[:, :, 0]
    cos, sin = [], []
    for axis in ((tok // GRID_W), (tok % GRID_W)):
        ang = (axis.astype(np.float32)[..., None] * inv_freq).astype(np.float32)
        cos += [np.cos(ang), np.cos(ang)]
        sin += [-np.sin(ang), np.sin(ang)]
    t[:, C_COS:C_COS + NT * HD] = np.concatenate(cos, -1).reshape(P, -1)
    t[:, C_SIN:C_SIN + NT * HD] = np.concatenate(sin, -1).reshape(P, -1)
    t[:, C_REV4:C_REV4 + GROUPS] = np.arange(GROUPS, 0, -1)[None]
    t[:, C_REV32:C_REV32 + EXPERTS] = np.arange(EXPERTS, 0, -1)[None]
    t[:, C_BASE:C_BASE + EXPERTS] = SLOTS * np.arange(EXPERTS)[None]
    return t


def slope(i):
    return float(np.float32(2.0 ** (-8.0 * (i + 1) / HEADS)))


def first_unit(layer, part):
    at = 0 if layer == 0 else SLABS[0] + OUTS + PER_ROUND
    return at + {"in": 0, "out": SLABS[layer], "experts": SLABS[layer] + OUTS}[part]


def hybrid_moe_kernel(nc, x_d, mix_norm, ffn_norm, ab_w_in, a_q_norm, a_k_norm, b_q_norm, b_k_norm, b_sink,
                      ab_w_out, c_w_in, c_q_norm, c_k_norm, c_w_out, moe_group_w, moe_group_b, moe_expert_w,
                      moe_expert_b, moe_w_gate, moe_w_up, moe_w_down, cst_d, out_d):
    with ExitStack() as ctx:
        def sb(name, shape, dt=F32):
            return ctx.enter_context(nc.sbuf_tensor(name, shape, dt))

        def sem(name):
            return ctx.enter_context(nc.semaphore(name))

        ring = [sb(f"ring{i}", [P, UNIT]) for i in range(RING)]
        x = sb("x", [P, NT, D])
        tokens = sb("tokens", [P, NT, NC, P])
        tokT = sb("tokT", [P, NC, SEQ])
        cst = sb("cst", [P, C_KEEP])
        area = sb("area", [P, 20 * SEQ + NT * 640 + 2 * HALF])
        work = sb("work", [P, 6 * HALF])
        router_w = sb("router_w", [P, 2, NC, NR])
        router_b = sb("router_b", [P, 2, NR])
        gains = sb("gains", [P, 4, NC])
        head_g = sb("head_g", [P, 4])
        gq_bc = sb("gq_bc", [P, HD])
        gk_bc = sb("gk_bc", [P, HD])
        rope = sb("rope", [P, 4, NT, HD])
        sink = sb("sink", [P, B_HEADS])
        neg_sink = sb("neg_sink", [P, B_HEADS])
        sumsq = sb("sumsq", [P, NT])
        mean = sb("mean", [P, NT])
        rstd = sb("rstd", [P, NT])
        newton = sb("newton", [P, 2, NT * 4])
        head_ss = sb("head_ss", [P, NT * 4])
        head_rs = sb("head_rs", [P, NT * 4])
        negmax = sb("negmax", [P, 2, NT])
        rowsum = sb("rowsum", [P, 2, NT])
        rowinv = sb("rowinv", [P, 2, NT])
        sink_e = sb("sink_e", [P, 2, NT])
        logit = sb("logit", [P, NT, NR])
        r_g = sb("r_g", [P, 6, NT, GROUPS])
        r_s = sb("r_s", [P, 12, NT])
        rank = sb("rank", [P, 2, NT])
        first_slot = sb("first_slot", [P, 2, NT])
        slot = sb("slot", [P, 2, NT])
        inside = sb("inside", [P, 2, 2, NT])
        weight = sb("weight", [P, 2, NT])
        most_i = sb("most_i", [1, 1], I32)
        most_f = sb("most_f", [1, 1])
        banks = ctx.enter_context(nc.psum_tensor("banks", [P, 8, HALF], F32))

        HT_TILES = 20
        headsT = area[:, 0:HT_TILES * SEQ].rearrange("p (n t) -> p n t", t=SEQ)
        KEYS = 8
        VW = 640
        v0 = HT_TILES * SEQ
        values = area[:, v0:v0 + NT * VW].rearrange("p (t n) -> p t n", t=NT)
        bias = area[:, v0 + NT * VW:v0 + NT * VW + 2 * HALF].rearrange("p (b t k) -> p b t k", b=2, t=NT)
        raw_gw = area[:, 0:2 * NC * GROUPS].rearrange("p (l n) -> p l n", l=2)
        raw_ew = area[:, 64:64 + 2 * NC * EXPERTS].rearrange("p (l g n) -> p l g n", l=2, g=GROUPS)
        raw_rope = area[:, 576:576 + 2 * NT * HD]
        gathered = area[:, 0:2 * NC * P].rearrange("p (b c s) -> p b c s", b=2, c=NC)
        outputs = area[:, 2048:2048 + D]
        onehot = area[:, 3072:3072 + 2 * NT * P].rearrange("p (b t s) -> p b t s", b=2, t=NT)
        weighted = area[:, 3584:3584 + NT * P].rearrange("p (t s) -> p t s", t=NT)
        weighted2 = area[:, 3840:3840 + NT * P].rearrange("p (t s) -> p t s", t=NT)
        scatter = area[:, 4096:4096 + NT * P]
        silu = area[:, 4352:4352 + DFF]
        hidden = area[:, 4608:4608 + DFF]
        hiddenT = area[:, 4864:4864 + 2 * P].rearrange("p (k s) -> p k s", k=2)
        r_e = area[:, 5120:5120 + 8 * NT * EXPERTS].rearrange("p (i t e) -> p i t e", i=8, t=NT)

        def work3(i):
            return work[:, 2 * i * HALF:2 * (i + 1) * HALF]

        square = work3(0).rearrange("p (b n) -> p b n", b=2)
        normed = work3(1).rearrange("p (b n) -> p b n", b=2)
        rot = work3(2).rearrange("p (b n) -> p b n", b=2)
        prob = work3(0).rearrange("p (b t k) -> p b t k", b=2, t=NT)
        score = work3(1).rearrange("p (b t k) -> p b t k", b=2, t=NT)
        probT = work3(2).rearrange("p (b c q) -> p b c q", b=2, c=NT)
        attT = tokT
        ident = cst[:, C_IDENT:C_IDENT + P]
        tri = cst[:, C_TRI:C_TRI + P]
        ones = cst[:, C_ONES:C_ONES + P]
        iota = cst[:, C_IOTA:C_IOTA + P]

        def bank(i):
            return banks[:, i, :]

        def bank2(i, a):
            return banks[:, i, :].rearrange("p (a b) -> p a b", a=a)

        Y_MIX = [[6, 7], [0, 1]]
        Y_MOE = [[4, 5], [6, 7]]

        s_x = sem("x_loaded")
        s_first = sem("first_constants_loaded")
        s_small = sem("small_inputs_loaded")
        s_unit = [sem(f"unit_loaded{i}") for i in range(RING)]
        s_used = sem("units_used")
        s_prep = sem("pool_prepared")
        s_pchain = sem("pool_chain")
        s_bias = sem("bias_ready")
        s_tail = sem("tail_cleared")
        s_dve = sem("dve_chain")
        s_x0 = sem("x_updated")
        s_sq = sem("act_square_sum")
        s_tok = sem("tokens_normalised")
        s_tokT_ps = sem("tokT_in_psum")
        s_tokT_a = sem("tokT_by_act")
        s_tokT_v = sem("tokT_by_dve")
        s_sqh = sem("head_squares")
        s_slab = sem("slab_taken")
        s_val = sem("values_taken")
        s_hT_ps = sem("headT_in_psum")
        s_hT = sem("headT_ready")
        s_sc_ps = sem("scores_in_psum")
        s_sc = sem("scores_max_ready")
        s_p = sem("prob_ready")
        s_pT_ps = sem("probT_in_psum")
        s_pT = sem("probT_ready")
        s_sink = sem("sink_term")
        s_norm = sem("prob_normalised")
        s_pv_ps = sem("attT_in_psum")
        s_att = sem("attT_ready")
        s_rl_ps = sem("router_logits")
        s_rd = sem("router_differences")
        s_re = sem("router_exponentials")
        s_pick = sem("experts_picked")
        s_pos_ps = sem("ranks_in_psum")
        s_most = sem("largest_count_ready")
        s_zero = sem("keys_cleared")

        class Signals:

            def __init__(self, name):
                self.unit = s_unit if name == "main" else [sem(f"extra_unit{i}") for i in range(RING)]
                self.used = s_used if name == "main" else sem("extra_units_used")
                self.slots = sem(name + "_slots_ready")
                self.chain = sem(name + "_batch_chain")
                self.onehot = sem(name + "_onehot_ready")
                self.weighted = sem(name + "_weighted_ready")
                self.gather_ps = sem(name + "_gathered_in_psum")
                self.gather = sem(name + "_gathered_ready")
                self.scatter_ps = sem(name + "_scatter_in_psum")
                self.scatter = sem(name + "_scatter_ready")
                self.silu = sem(name + "_silu_ready")
                self.hidden = sem(name + "_hidden_ready")
                self.hiddenT_ps = sem(name + "_hiddenT_in_psum")
                self.hiddenT = sem(name + "_hiddenT_ready")
                self.out_ps = sem(name + "_first_half_in_psum")
                self.out_a = sem(name + "_outputs_by_act")
                self.out_v = sem(name + "_outputs_by_dve")
                self.y_ps = sem(name + "_sums_in_psum")
                self.added = sem(name + "_sums_added")
                self.by_pe = [(self.gather_ps, 2), (self.scatter_ps, 1), (self.hiddenT_ps, 1), (self.out_ps, 1),
                              (self.y_ps, 2 * NT)]
                self.by_act = [(self.scatter, 1), (self.silu, 1), (self.hiddenT, 1), (self.out_a, 1)]
                self.by_dve = [(self.chain, 8), (self.onehot, 1), (self.weighted, 1), (self.gather, 2),
                               (self.hidden, 1), (self.out_v, 1), (self.added, 1)]

        main, extra = Signals("main"), Signals("extra")
        s_done = sem("output_stored")

        def loaded(n):
            return 16 * (n // RING + 1)

        class Round:

            def __init__(self, sig, layer, first_batch, unit0, turns):
                self.sig, self.layer, self.first = sig, layer, first_batch
                self.unit0, self.turns = unit0, turns

            def batches_before(self, step, place):
                return self.first + (LOOP * step + place)

            def ring_slot(self, place, stage, j):
                return (self.unit0 + PER_BATCH * place + STAGE * stage + j) % RING

            def unit_loaded(self, step, place, stage, j):
                k = self.unit0 + PER_BATCH * place + STAGE * stage + j
                return 16 * (k // RING + 1) + 16 * (LOOP * PER_BATCH // RING) * step + 16 * self.turns

            def units_used(self, step, place, stage):
                return (self.unit0 + PER_BATCH * place + STAGE * (stage + 1)) + LOOP * PER_BATCH * step \
                    + RING * self.turns

        PER_SLOTS = 6

        def residual_ready(eng, m):
            if m == 0:
                eng.wait_ge(s_x, 16 * NT)
            elif m % 2:
                eng.wait_ge(s_x0, NT * (m + 1) // 2)
            else:
                eng.wait_ge(main.added, BATCHES * m // 2 + 1)
                eng.wait_ge(extra.added, (ROUNDS - 1) * BATCHES * m // 2 + 1)

        def over_batches(eng, body):
            with eng.Fori(0, BATCHES // LOOP) as step:
                for place in range(LOOP):
                    body(step, place)

        def start_signals(eng, *signals):
            for per_batch in signals:
                for s, count in per_batch:
                    eng.sem_inc(s, count)

        def all_rounds(eng, layer, one_round, counts, after=None):
            one_round(Round(main, layer, BATCHES * layer + 1, first_unit(layer, "experts"), 0), 0)
            eng.wait_ge(s_most, layer + 1)
            most = eng.value_load(most_i[0:1, 0:1], min_val=0, max_val=SEQ)
            with eng.If(most > SLOTS):
                with eng.Fori(1, ROUNDS) as rnd:
                    before = (ROUNDS - 1) * layer - 1 + rnd
                    one_round(Round(extra, layer, before * BATCHES + 1, 0, before * (PER_ROUND // RING) + 1), rnd)
                if after:
                    after()
            with eng.Else():
                for s, count in counts:
                    eng.sem_inc(s, (ROUNDS - 1) * count)

        def per_round(per_batch):
            return [(s, BATCHES * count) for s, count in per_batch]

        def head_place(layer, h):
            if layer == 1:
                return h // 2, KEYS + 2 * (h // 4) + h % 2, HD * (h // 4)
            if h < A_HEADS:
                return h // 2, KEYS + h, HD * h
            return h // 2, KEYS + A_HEADS + 2 * ((h - 8) // 4) + h % 2, 512 + HD * ((h - 8) // 4)

        SLAB_PLAN = [
            [("heads", 0, 0), ("heads", 2, 0), ("keys", KEYS, 1), ("keys", KEYS + 4, 1), ("values", 0, None),
             ("values", 256, None), ("heads", 4, 2), ("heads", 6, 2), ("shared2", KEYS + 8, 3)],
            [("heads", 0, "q"), ("heads", 2, "q"), ("heads", 4, "q"), ("heads", 6, "q"),
             ("shared4", KEYS, "k"), ("values", 0, None)],
        ]
        TURNS = [[], []]
        for lay in range(2):
            for s, (kind, tile, g) in enumerate(SLAB_PLAN[lay]):
                if kind in ("heads", "keys", "shared2"):
                    TURNS[lay].append((s, tile, g, 0))
                elif kind == "shared4":
                    TURNS[lay] += [(s, tile, g, 0), (s, tile + 4, g, 1)]

        def turns_before(layer, slab):
            return (len(TURNS[0]) if layer else 0) + sum(t[0] < slab for t in TURNS[layer])

        def norm_slabs_before(layer, slab):
            n = sum(k != "values" for k, _, _ in SLAB_PLAN[0]) if layer else 0
            return n + sum(k != "values" for k, _, _ in SLAB_PLAN[layer][:slab])

        NORMED = [(lay, s) for lay in range(2) for s in range(SLABS[lay]) if SLAB_PLAN[lay][s][0] != "values"]

        def values_before(layer, slab):
            n = sum(k in ("values", "shared2") for k, _, _ in SLAB_PLAN[0]) if layer else 0
            return n + sum(k in ("values", "shared2") for k, _, _ in SLAB_PLAN[layer][:slab])

        def head_rows(layer, s, k, part):
            if SLAB_PLAN[layer][s][0] == "shared4":
                return normed[:, part, :].rearrange("p (t n) -> p t n", t=NT)
            return normed[:, k, :].rearrange("p (t n) -> p t n", t=NT)

        block = ctx.enter_context(nc.Block())

        @block.sync
        def _(sp):
            for u in extra.unit:
                sp.sem_inc(u, 16)
            for t in range(NT):
                sp.dma_start(x[:, t, :], x_d[0, t * P:(t + 1) * P, :]).then_inc(s_x, 16)
            sp.dma_start(cst[:, C_IDENT:C_IDENT + P], cst_d[:, C_IDENT:C_IDENT + P]).then_inc(s_first, 16)
            for m in range(2):
                sp.dma_start(gains[:, m:4:2, :], (mix_norm, ffn_norm)[m].rearrange("l (p c) -> p l c", c=NC))\
                    .then_inc(s_first, 16)

            def room(n):
                if n >= RING:
                    sp.wait_ge(s_used, n - RING + 1)

            def load_in(layer, s):
                w_in = (ab_w_in, c_w_in)[layer][0].rearrange("(p c) n -> p c n", c=NC)
                n = first_unit(layer, "in") + s
                room(n)
                sp.dma_start(ring[n % RING][:, :].rearrange("p (c n) -> p c n", c=NC),
                             w_in[:, :, 256 * s:256 * s + 256]).then_inc(s_unit[n % RING], 16)

            def load_small():
                sp.dma_start(cst[:, P:C_KEEP], cst_d[:, P:C_KEEP]).then_inc(s_small, 16)
                sp.dma_start(raw_rope, cst_d[:, C_KEEP:C_ALL]).then_inc(s_small, 16)
                for c, g in enumerate((a_q_norm, a_k_norm, b_q_norm, b_k_norm)):
                    for r in range(2):
                        sp.dma_start(head_g[r * HD:(r + 1) * HD, c:c + 1], g[0].rearrange("(p c) -> p c", c=1))\
                            .then_inc(s_small, 16)
                sp.dma_start(gq_bc[:, :], c_q_norm[0].partition_broadcast(P)).then_inc(s_small, 16)
                sp.dma_start(gk_bc[:, :], c_k_norm[0].partition_broadcast(P)).then_inc(s_small, 16)
                sp.dma_start(sink[:, :], b_sink[0].partition_broadcast(P)).then_inc(s_small, 16)
                sp.dma_start(raw_gw, moe_group_w.rearrange("l (p c) g -> p l (c g)", c=NC)).then_inc(s_small, 16)
                for l in range(2):
                    sp.dma_start(raw_ew[:, l, :, :], moe_expert_w[l].rearrange("g (p c) e -> p g (c e)", c=NC))\
                        .then_inc(s_small, 16)
                    sp.dma_start(router_b[:, l, 0:GROUPS], moe_group_b[l].partition_broadcast(P)).then_inc(s_small, 16)
                    sp.dma_start(router_b[:, l, GROUPS:NR],
                                 moe_expert_b[l].rearrange("g e -> (g e)").partition_broadcast(P)).then_inc(s_small, 16)

            for layer in range(2):
                for s in range(SLABS[layer]):
                    load_in(layer, s)
                    if layer == 0 and s == 1:
                        load_small()
                w_out = (ab_w_out, c_w_out)[layer][0]
                for s in range(OUTS):
                    n = first_unit(layer, "out") + s
                    room(n)
                    sp.dma_start(ring[n % RING][:, :].rearrange("p (c n) -> p c n", c=2),
                                 w_out[256 * s:256 * s + 256, :].rearrange("(c p) n -> p c n", p=P))\
                        .then_inc(s_unit[n % RING], 16)
                gate = moe_w_gate[layer].rearrange("g e (p c) f -> (g e) p (c f)", c=NC)
                up = moe_w_up[layer].rearrange("g e (p c) f -> (g e) p (c f)", c=NC)
                down = moe_w_down[layer].rearrange("g e (c p) n -> (g e) p c n", p=P)

                def load_round(rd, rnd):
                    sig = rd.sig
                    if sig is extra:
                        sp.wait_ge(s_used, first_unit(layer, "experts") + PER_ROUND)
                        sp.wait_ge(sig.used, RING * rd.turns)
                    for b in range(BATCHES):
                        for stage, w in enumerate((gate, up, down)):
                            for j in range(STAGE):
                                k = rd.unit0 + PER_BATCH * b + STAGE * stage + j
                                if k >= RING:
                                    sp.wait_ge(sig.used, RING * rd.turns + k - RING + 1)
                                e = BATCH * b + j
                                if stage < 2:
                                    src, dst = w[e], ring[k % RING][:, :]
                                else:
                                    src, dst = w[e], ring[k % RING][:, :].rearrange("p (c n) -> p c n", c=2)
                                sp.dma_start(dst, src).then_inc(sig.unit[k % RING], 16)

                def last_used():
                    sp.wait_ge(extra.used, (ROUNDS - 1) * PER_ROUND * (layer + 1) + RING)

                all_rounds(sp, layer, load_round, [(u, 16 * PER_ROUND // RING) for u in extra.unit], last_used)
            sp.wait_ge(main.added, 2 * BATCHES + 1)
            sp.wait_ge(extra.added, 2 * (ROUNDS - 1) * BATCHES + 1)
            for t in range(NT):
                sp.dma_start(out_d[0, t * P:(t + 1) * P, :], x[:, t, :]).then_inc(s_done, 16)
            sp.wait_ge(s_done, 16 * NT)

        SMALL = 2 + 8 + 3 + 1 + 2 * 3

        @block.gpsimd
        def _(pool):
            n = [0]

            def link(ins):
                n[0] += 1
                ins.then_inc(s_pchain, 1)
                pool.wait_ge(s_pchain, n[0])

            pool.wait_ge(s_first, 48)
            pool.wait_ge(s_small, 16 * SMALL)
            for c in (0, 2):
                link(nc.gpsimd.tensor_scalar(head_g[:, c:c + 1], head_g[:, c:c + 1], -1.0, None, ALU.mult))
            for c in (1, 3):
                link(nc.gpsimd.tensor_scalar(head_g[:, c:c + 1], head_g[:, c:c + 1], 8.0, None, ALU.mult))
            nc.gpsimd.tensor_scalar(neg_sink[:, :], sink[:, :], -1.0, None, ALU.mult).then_inc(s_prep, 1)

            def table(h):
                if h >= 2:
                    pool.wait_ge(s_sc, 2 * (h - 1))
                mask = (C_MA, C_MB)[h // A_HEADS]
                i = 2 * h if h < A_HEADS else 2 * (h - A_HEADS) + 1
                b = bias[:, h % 2, :, :].rearrange("p t k -> p (t k)")
                link(nc.gpsimd.tensor_scalar(b, cst[:, C_DIST:C_DIST + HALF], slope(i), None, ALU.mult))
                nc.gpsimd.tensor_tensor(b, b, cst[:, mask:mask + HALF], ALU.add).then_inc(s_bias, 1)

            keys = area[:, KEYS * SEQ:HT_TILES * SEQ]
            nc.gpsimd.memset(keys, 0.0).then_inc(s_zero, 1)
            for h in range(2):
                table(h)
            for layer in range(2):
                nc.gpsimd.tensor_copy(router_w[:, layer, :, 0:GROUPS],
                                      raw_gw[:, layer, :].rearrange("p (c g) -> p c g", c=NC)).then_inc(s_prep, 1)
                for g in range(GROUPS):
                    a = GROUPS + g * PER_GROUP
                    nc.gpsimd.tensor_copy(router_w[:, layer, :, a:a + PER_GROUP],
                                          raw_ew[:, layer, g, :].rearrange("p (c e) -> p c e", c=NC))\
                        .then_inc(s_prep, 1)
            for i, (g, scale) in enumerate(((gq_bc, -1.0), (gk_bc, 8.0))):
                link(nc.gpsimd.tensor_scalar(g[:, :], g[:, :], scale, None, ALU.mult))
                for t in range(NT):
                    nc.gpsimd.tensor_tensor(rope[:, 2 * i, t, :], raw_rope[:, HD * t:HD * t + HD],
                                            g[:, :], ALU.mult).then_inc(s_prep, 1)
                    for b in range(2):
                        sin_v = raw_rope[:, HD * (NT + t):HD * (NT + t + 1)].rearrange("p (a b j) -> p a b j", a=2, b=2)
                        nc.gpsimd.tensor_tensor(
                            rope[:, 2 * i + 1, t, :].rearrange("p (a b j) -> p a b j", a=2, b=2)[:, :, b, :],
                            sin_v[:, :, b, :],
                            g[:, :].rearrange("p (a b j) -> p a b j", a=2, b=2)[:, :, 1 - b, :],
                            ALU.mult).then_inc(s_prep, 1)
            for h in range(2, HEADS):
                table(h)
            pool.wait_ge(s_tok, NT * 3)
            nc.gpsimd.memset(keys, 0.0).then_inc(s_zero, 1)

        PREP = 1 + 2 * (1 + GROUPS) + 2 * NT * 3

        @block.tensor
        def _(pe):
            def transpose_tokens(m):
                if m == 0:
                    pe.wait_ge(s_first, 48)
                for pair in range(NC // 2):
                    for c in range(2):
                        for t in range(NT):
                            if pair == 0 and c == 0:
                                pe.wait_ge(s_tok, NT * m + t + 1)
                            a = (c * NT + t) * P
                            ins = pe.transpose(bank(2 + pair)[:, a:a + P], tokens[:, t, 2 * pair + c, :], ident)
                    ins.then_inc(s_tokT_ps, 1)

            def tokT_ready(m):
                pe.wait_ge(s_tokT_a, 4 * (m + 1))
                pe.wait_ge(s_tokT_v, 2 * (m + 1))

            def slab(layer, s):
                n = first_unit(layer, "in") + s
                g = s + SLABS[0] * layer
                if s >= 2:
                    pe.wait_ge(s_slab, norm_slabs_before(layer, s - 1))
                    pe.wait_ge(s_val, values_before(layer, s - 1))
                pe.wait_ge(s_unit[n % RING], loaded(n))
                w = ring[n % RING][:, :].rearrange("p (c n) -> p c n", c=NC)
                for t in range(NT):
                    for c in range(NC):
                        ins = pe.matmul(bank2(s % 2, NT)[:, t, :], tokT[:, c, t * P:(t + 1) * P], w[:, c, :],
                                        start=(c == 0), stop=(c == NC - 1))
                ins.then_inc(s_used, 1)

            def turn_heads(layer, s):
                done = turns_before(layer, s)
                for (ts, tile, g, part) in TURNS[layer]:
                    if ts != s:
                        continue
                    b = done % 2
                    pe.wait_ge(s_slab, norm_slabs_before(layer, s) + 1)
                    if done >= 2:
                        pe.wait_ge(s_hT, done - 1)
                    k = norm_slabs_before(layer, s) % 2
                    for c in range(2):
                        for t in range(NT):
                            src = head_rows(layer, s, k, part)[:, t, c * P:(c + 1) * P]
                            ins = pe.transpose(bank2(2 + b, 2)[:, c, t * P:(t + 1) * P], src, ident)
                    ins.then_inc(s_hT_ps, 1)
                    done += 1

            def scores(layer, h):
                g = HEADS * layer + h
                qt, kt, _ = head_place(layer, h)
                if h == 0:
                    pe.wait_ge(s_hT, turns_before(layer, SLABS[layer]))
                    pe.wait_ge(s_val, values_before(layer, SLABS[layer]))
                if h >= 2:
                    if layer == 0:
                        pe.wait_ge(s_sc, NT * (g - 1))
                    else:
                        pe.wait_ge(s_p, g - 1)
                for t in range(NT):
                    ins = pe.matmul(bank2(h % 2, NT)[:, t, :], headsT[:, qt, t * P:(t + 1) * P],
                                    headsT[:, kt, :], start=True, stop=True)
                ins.then_inc(s_sc_ps, 1)

            def turn_prob(layer, h):
                g = HEADS * layer + h
                pe.wait_ge(s_norm, g + 1)
                if h >= 2:
                    pe.wait_ge(s_pT, g - 1)
                for c in range(NT):
                    for t in range(NT):
                        ins = pe.transpose(bank2(2 + h % 2, NT)[:, c, t * P:(t + 1) * P],
                                           prob[:, h % 2, t, c * P:(c + 1) * P], ident)
                ins.then_inc(s_pT_ps, 1)

            def prob_values(layer, i):
                pe.wait_ge(s_pT, HEADS * layer + 2 * i + 2)
                if i >= 2:
                    pe.wait_ge(s_att, HEADS // 2 * layer + i - 1)
                for c in range(NT):
                    for r in range(2):
                        vcol = head_place(layer, 2 * i + r)[2]
                        ins = pe.matmul(bank(4 + i % 2)[r * HD:(r + 1) * HD, 0:SEQ], values[:, c, vcol:vcol + HD],
                                        probT[:, r, c, :], start=(c == 0), stop=(c == NT - 1))
                ins.then_inc(s_pv_ps, 1)

            def project_out(layer, u):
                n = first_unit(layer, "out") + u
                pe.wait_ge(s_att, HEADS // 2 * layer + 2 * u + 2)
                pe.wait_ge(s_unit[n % RING], loaded(n))
                w = ring[n % RING][:, :].rearrange("p (c n) -> p c n", c=2)
                for t in range(NT):
                    for half in range(2):
                        for c in range(2):
                            k = 2 * u + c
                            ins = pe.matmul(bank(Y_MIX[t][half]), attT[:, k, t * P:(t + 1) * P],
                                            w[:, c, half * HALF:(half + 1) * HALF],
                                            start=(k == 0), stop=(k == NC - 1))
                ins.then_inc(s_used, 1)

            def router(layer):
                if layer == 0:
                    pe.wait_ge(s_prep, PREP)
                for t in range(NT):
                    for c in range(NC):
                        ins = pe.matmul(bank(6)[:, t * NR:(t + 1) * NR], tokT[:, c, t * P:(t + 1) * P],
                                        router_w[:, layer, c, :], start=(c == 0), stop=(c == NC - 1))
                ins.then_inc(s_rl_ps, 1)
                pe.wait_ge(s_pick, layer + 1)
                picked = r_e[:, 7, :, :]
                for t in range(NT):
                    pe.matmul(bank(1)[:, 0:EXPERTS], ones, picked[:, t, :], start=(t == 0), stop=(t == NT - 1))
                for t in range(NT):
                    o = bank(0)[:, t * EXPERTS:(t + 1) * EXPERTS]
                    for b in range(t):
                        pe.matmul(o, ones, picked[:, b, :], start=(b == 0), stop=False)
                    ins = pe.matmul(o, tri, picked[:, t, :], start=(t == 0), stop=True)
                ins.then_inc(s_pos_ps, 1)

            def experts(rd, rnd):
                sig, layer = rd.sig, rd.layer
                if sig is extra:
                    pe.wait_ge(main.added, BATCHES * (layer + 1) + 1)
                else:
                    pe.wait_ge(s_most, layer + 1)

                def batch(step, place):
                    g = rd.batches_before(step, place)

                    def arrived(stage):
                        for j in range(STAGE):
                            pe.wait_ge(sig.unit[rd.ring_slot(place, stage, j)], rd.unit_loaded(step, place, stage, j))

                    pe.wait_ge(sig.onehot, g + 1)
                    pe.wait_ge(sig.added, g)
                    for c in range(NC):
                        for t in range(NT):
                            ins = pe.matmul(bank(4 + c // 4)[:, c % 4 * P:(c % 4 + 1) * P], tokens[:, t, c, :],
                                            onehot[:, 0, t, :], start=(t == 0), stop=(t == NT - 1))
                        if c % 4 == 3:
                            ins.then_inc(sig.gather_ps, 1)
                    pe.wait_ge(sig.weighted, g + 1)
                    for t in range(NT):
                        ins = pe.transpose(bank(7)[:, t * P:(t + 1) * P], weighted[:, t, :], ident)
                    ins.then_inc(sig.scatter_ps, 1)
                    pe.wait_ge(sig.gather, 2 * (g + 1))
                    pe.wait_ge(sig.hidden, g)
                    for stage in range(2):
                        arrived(stage)
                        for c in range(NC):
                            for j in range(BATCH):
                                w = ring[rd.ring_slot(place, stage, j)][:, :].rearrange("p (c n) -> p c n", c=NC)
                                ins = pe.matmul(bank(stage)[j * SLOTS:(j + 1) * SLOTS, 0:DFF],
                                                gathered[:, 0, c, j * SLOTS:(j + 1) * SLOTS], w[:, c, :],
                                                start=(c == 0), stop=(c == NC - 1))
                        ins.then_inc(sig.used, STAGE)
                    pe.wait_ge(sig.hidden, g + 1)
                    for k in range(2):
                        ins = pe.transpose(bank(6)[:, k * P:(k + 1) * P], hidden[:, k * P:(k + 1) * P], ident)
                    ins.then_inc(sig.hiddenT_ps, 1)
                    pe.wait_ge(sig.hiddenT, g + 1)
                    pe.wait_ge(sig.out_a, g)
                    pe.wait_ge(sig.out_v, g)
                    arrived(2)
                    for half in range(2):
                        for k in range(2):
                            for j in range(BATCH):
                                w = ring[rd.ring_slot(place, 2, j)][:, :].rearrange("p (c n) -> p c n", c=2)
                                ins = pe.matmul(bank(2 + half)[j * SLOTS:(j + 1) * SLOTS, :],
                                                hiddenT[:, k, j * SLOTS:(j + 1) * SLOTS],
                                                w[:, k, half * HALF:(half + 1) * HALF],
                                                start=(k == 0), stop=(k == 1))
                        if half == 0:
                            ins.then_inc(sig.out_ps, 1)
                        else:
                            ins.then_inc(sig.used, STAGE)
                    pe.wait_ge(sig.scatter, g + 1)
                    for half in range(2):
                        pe.wait_ge((sig.out_a, sig.out_v)[half], g + 1)
                        for t in range(NT):
                            pe.matmul(bank(Y_MOE[t][half]), scatter[:, t * P:(t + 1) * P],
                                      outputs[:, half * HALF:(half + 1) * HALF],
                                      start=True, stop=True).then_inc(sig.y_ps, 1)

                over_batches(pe, batch)

            start_signals(pe, main.by_pe, extra.by_pe)
            pe.sem_inc(extra.used, RING)
            for layer in range(2):
                transpose_tokens(2 * layer)
                tokT_ready(2 * layer)
                for s in range(SLABS[layer] + 1):
                    if s < SLABS[layer]:
                        slab(layer, s)
                    if s >= 1:
                        turn_heads(layer, s - 1)
                for h in range(HEADS + 2):
                    if h < HEADS:
                        scores(layer, h)
                    if h >= 3 and h % 2 == 1:
                        prob_values(layer, (h - 3) // 2)
                    if 1 <= h <= HEADS:
                        turn_prob(layer, h - 1)
                for u in range(OUTS):
                    project_out(layer, u)
                transpose_tokens(2 * layer + 1)
                tokT_ready(2 * layer + 1)
                router(layer)
                all_rounds(pe, layer, experts, [(extra.used, PER_ROUND)] + per_round(extra.by_pe))

        @block.scalar
        def _(act):
            def square_sum(m):
                residual_ready(act, m)
                nc.scalar.activation(work3(0), x[:, 0, :], ACT.Square,
                                     accum_out=sumsq[:, 0:1]).then_inc(s_sq, 1)

            def take_tokT(m):
                if m == 0:
                    act.wait_ge(s_first, 48)
                for pair in (0, 2):
                    act.wait_ge(s_tokT_ps, 4 * m + pair + 1)
                    for c in range(2):
                        k = 2 * pair + c
                        nc.scalar.activation(tokT[:, k, :], bank2(2 + pair, 2)[:, c, :], ACT.Copy,
                                             scale=gains[:, m, k:k + 1]).then_inc(s_tokT_a, 1)

            def slab(layer, s):
                kind, col, _ = SLAB_PLAN[layer][s]
                act.wait_ge(s_used, first_unit(layer, "in") + s + 1)
                ps = bank2(s % 2, NT)
                if kind == "values":
                    nc.scalar.activation(values[:, :, col:col + 256], ps, ACT.Copy).then_inc(s_val, 1)
                    return
                i = norm_slabs_before(layer, s)
                w = 2 * HD if kind == "shared2" else 4 * HD
                if kind == "shared2":
                    nc.scalar.activation(values[:, :, 512:640], ps[:, :, w:2 * w], ACT.Copy).then_inc(s_val, 1)
                if i >= 2:
                    act.wait_ge(s_slab, i - 1)
                nc.scalar.activation(square[:, i % 2, 0:NT * w].rearrange("p (t n) -> p t n", t=NT), ps[:, :, 0:w],
                                     ACT.Square).then_inc(s_sqh, 1)

            def take_heads(layer, s):
                i = turns_before(layer, s)
                for (ts, tile, g, part) in TURNS[layer]:
                    if ts != s:
                        continue
                    act.wait_ge(s_hT_ps, i + 1)
                    if i == 0:
                        act.wait_ge(s_prep, PREP)
                    scale = 1.0 if layer else head_g[:, g:g + 1]
                    ps = bank2(2 + i % 2, 2)
                    if tile < KEYS:
                        nc.scalar.activation(headsT[:, tile:tile + 2, :], ps, ACT.Copy, scale=scale).then_inc(s_hT, 1)
                    else:
                        act.wait_ge(s_zero, layer + 1)
                        for r in range(2):
                            rows = slice(r * HD, (r + 1) * HD)
                            ins = nc.scalar.activation(headsT[rows, tile + r:tile + 4:2, :], ps[rows, :, :], ACT.Copy,
                                                       scale=1.0 if layer else head_g[rows, g:g + 1])
                        ins.then_inc(s_hT, 1)
                    i += 1

            def exponentials(layer, h):
                g = HEADS * layer + h
                act.wait_ge(s_sc, NT * (g + 1))
                if h >= 2:
                    act.wait_ge(s_pT_ps, g - 1)
                for t in range(NT):
                    src = score[:, h % 2, t, :] if layer == 0 else bank2(h % 2, NT)[:, t, :]
                    ins = nc.scalar.activation(prob[:, h % 2, t, :], src, ACT.Exp, scale=-1.0,
                                               bias=negmax[:, h % 2, t:t + 1], accum_out=rowsum[:, h % 2, t:t + 1])
                if layer == 0 and h >= A_HEADS:
                    k = h - A_HEADS
                    ins = nc.scalar.activation(sink_e[:, h % 2, :], negmax[:, h % 2, :], ACT.Exp,
                                               bias=sink[:, k:k + 1])
                ins.then_inc(s_p, 1)

            def take_probT(layer, h):
                g = HEADS * layer + h
                act.wait_ge(s_pT_ps, g + 1)
                act.wait_ge(s_pv_ps, HEADS // 2 * layer + h // 2)
                nc.scalar.activation(probT[:, h % 2, :, :], bank2(2 + h % 2, NT), ACT.Copy).then_inc(s_pT, 1)

            def take_att(layer, i):
                act.wait_ge(s_pv_ps, HEADS // 2 * layer + i + 1)
                nc.scalar.activation(attT[:, i, :], bank(4 + i % 2)[:, 0:SEQ], ACT.Copy).then_inc(s_att, 1)

            def router(layer):
                act.wait_ge(s_rd, 2 * layer + 1)
                nc.scalar.activation(r_g[:, 5, :, :], r_g[:, 4, :, :], ACT.Exp).then_inc(s_re, 1)
                act.wait_ge(s_rd, 2 * layer + 2)
                nc.scalar.activation(r_s[:, 6, :], r_s[:, 5, :], ACT.Exp).then_inc(s_re, 1)

            def experts(rd, rnd):
                sig = rd.sig

                def batch(step, place):
                    g = rd.batches_before(step, place)
                    act.wait_ge(sig.scatter_ps, g + 1)
                    nc.scalar.activation(scatter, bank(7)[:, 0:SEQ], ACT.Copy).then_inc(sig.scatter, 1)
                    act.wait_ge(sig.used, rd.units_used(step, place, 0))
                    act.wait_ge(sig.hidden, g)
                    nc.scalar.activation(silu, bank(0)[:, 0:DFF], ACT.Silu).then_inc(sig.silu, 1)
                    act.wait_ge(sig.hiddenT_ps, g + 1)
                    nc.scalar.activation(hiddenT, bank2(6, 4)[:, 0:2, :], ACT.Copy).then_inc(sig.hiddenT, 1)
                    act.wait_ge(sig.out_ps, g + 1)
                    nc.scalar.activation(outputs[:, 0:HALF], bank(2), ACT.Copy).then_inc(sig.out_a, 1)

                over_batches(act, batch)

            start_signals(act, main.by_act, extra.by_act)
            for layer in range(2):
                square_sum(2 * layer)
                take_tokT(2 * layer)
                for s in range(SLABS[layer] + 1):
                    if s < SLABS[layer]:
                        slab(layer, s)
                    if s >= 1:
                        take_heads(layer, s - 1)
                for h in range(HEADS + 2):
                    if h < HEADS:
                        exponentials(layer, h)
                    if h >= 3 and h % 2 == 1:
                        take_att(layer, (h - 3) // 2)
                    if 1 <= h <= HEADS:
                        take_probT(layer, h - 1)
                square_sum(2 * layer + 1)
                take_tokT(2 * layer + 1)
                router(layer)
                all_rounds(act, layer, experts, per_round(extra.by_act))

        @block.vector
        def _(dve):
            n = [0]
            V = nc.vector

            def link(ins):
                n[0] += 1
                ins.then_inc(s_dve, 1)
                dve.wait_ge(s_dve, n[0])

            def inverse_root(y, v, k):
                half, cube = newton[:, 0, 0:k], newton[:, 1, 0:k]
                link(V.tensor_scalar(half.bitcast(I32), v.bitcast(I32), 1, None, ALU.logical_shift_right))
                link(V.tensor_scalar(y.bitcast(I32), half.bitcast(I32), -1.0, float(0x5f3759df), ALU.mult, ALU.add))
                for _ in range(3):
                    link(V.tensor_tensor(half, y, y, ALU.mult))
                    link(V.scalar_tensor_tensor(cube, half, -0.5, v, ALU.mult, ALU.mult))
                    link(V.scalar_tensor_tensor(y, cube, 1.5, y, ALU.add, ALU.mult))

            def normalise(m):
                residual_ready(dve, m)
                link(V.tensor_tensor_reduce(work3(1), x[:, 1, :], x[:, 1, :],
                                            1.0, 0.0, ALU.mult, ALU.add, sumsq[:, 1:2]))
                dve.wait_ge(s_sq, m + 1)
                link(V.tensor_scalar(mean[:, :], sumsq[:, :], 1.0 / D, EPS, ALU.mult, ALU.add))
                inverse_root(rstd[:, :], mean[:, :], NT)
                for t in range(NT):
                    V.tensor_scalar(tokens[:, t, :, :], x[:, t, :].rearrange("q (p c) -> q c p", c=NC),
                                    rstd[:, t:t + 1], None, ALU.mult).then_inc(s_tok, 1)

            def take_tokT(m):
                if m == 0:
                    dve.wait_ge(s_first, 48)
                for pair in (1, 3):
                    dve.wait_ge(s_tokT_ps, 4 * m + pair + 1)
                    V.tensor_tensor(tokT[:, 2 * pair:2 * pair + 2, :], bank2(2 + pair, 2),
                                    gains[:, m, 2 * pair:2 * pair + 2].unsqueeze(2).to_broadcast([P, 2, SEQ]),
                                    ALU.mult).then_inc(s_tokT_v, 1)

            def slab(layer, s):
                kind, tile, g = SLAB_PLAN[layer][s]
                if kind == "values":
                    return
                i = norm_slabs_before(layer, s)
                nh = 2 if kind == "shared2" else 4
                w = nh * HD
                ps = bank2(s % 2, NT)[:, :, 0:w].rearrange("p t (h d) -> p t h d", d=HD)
                dve.wait_ge(s_sqh, i + 1)
                link(V.tensor_reduce(head_ss[:, 0:NT * nh],
                                     square[:, i % 2, 0:NT * w].rearrange("p (n d) -> p n d", d=HD), AX, ALU.add))
                link(V.tensor_scalar(head_ss[:, 0:NT * nh], head_ss[:, 0:NT * nh], HD * EPS, None, ALU.add))
                inverse_root(head_rs[:, 0:NT * nh], head_ss[:, 0:NT * nh], NT * nh)
                rs = head_rs[:, 0:NT * nh].rearrange("p (t h) -> p t h", t=NT).unsqueeze(3)\
                    .to_broadcast([P, NT, nh, HD])
                if i >= 2:
                    dve.wait_ge(s_hT_ps, turns_before(*NORMED[i - (kind != "shared4")]))
                if layer == 0:
                    dst = normed[:, i % 2, :].rearrange("p (t h d) -> p t h d", t=NT, d=HD)
                    if kind != "shared2":
                        V.tensor_tensor(dst, ps, rs, ALU.mult).then_inc(s_slab, 1)
                    else:
                        dup = normed[:, i % 2, :].rearrange("p (t h r d) -> p t h r d", t=NT, r=2, d=HD)
                        link(V.tensor_tensor(dup[:, :, :, 0, :], ps, rs, ALU.mult))
                        V.tensor_tensor(dup[:, :, :, 1, :], ps, rs, ALU.mult).then_inc(s_slab, 1)
                    return
                flat = square[:, i % 2, :]
                link(V.tensor_tensor(flat.rearrange("p (t h d) -> p t h d", t=NT, d=HD), ps, rs, ALU.mult))
                tab = 0 if g == "q" else 2

                def swap(v, b):
                    return v.rearrange("p (h a b j) -> p (h a) b j", a=2, b=2, j=16)[:, :, b, :]

                for t in range(NT):
                    q = flat[:, t * w:(t + 1) * w]
                    r0 = rot[:, 0, t * w:(t + 1) * w]
                    r1 = rot[:, 1, t * w:(t + 1) * w]
                    cosb = rope[:, tab, t, :].unsqueeze(1).to_broadcast([P, 4, HD])
                    V.tensor_tensor(r0.rearrange("p (h d) -> p h d", d=HD), q.rearrange("p (h d) -> p h d", d=HD),
                                    cosb, ALU.mult).then_inc(s_dve, 1)
                    n[0] += 1
                    for b in range(2):
                        for a in range(2):
                            sinb = rope[:, tab + 1, t, 32 * a + 16 * b:32 * a + 16 * b + 16].unsqueeze(1)\
                                .to_broadcast([P, 4, 16])
                            V.tensor_tensor(
                                r1.rearrange("p (h d) -> p h d", d=HD)[:, :, 32 * a + 16 * b:32 * a + 16 * b + 16],
                                q.rearrange("p (h d) -> p h d", d=HD)[:, :, 32 * a + 16 * (1 - b):
                                                                     32 * a + 16 * (1 - b) + 16],
                                sinb, ALU.mult).then_inc(s_dve, 1)
                            n[0] += 1
                dve.wait_ge(s_dve, n[0])
                if kind == "heads":
                    V.tensor_tensor(normed[:, i % 2, :], rot[:, 0, :], rot[:, 1, :], ALU.add).then_inc(s_slab, 1)
                else:
                    for part in range(2):
                        dst = normed[:, part, :].rearrange("p (t h r d) -> p t h r d", t=NT, r=2, d=HD)
                        for r in range(2):
                            a = [rot[:, k, :].rearrange("p (t n) -> p t n", t=NT)[:, :, part * 2 * HD:(part + 1) * 2 * HD]
                                 .rearrange("p t (h d) -> p t h d", d=HD) for k in range(2)]
                            ins = V.tensor_tensor(dst[:, :, :, r, :], a[0], a[1], ALU.add)
                            if part == 0 or r == 0:
                                link(ins)
                    ins.then_inc(s_slab, 1)

            def maxima(layer, h):
                g = HEADS * layer + h
                dve.wait_ge(s_sc_ps, g + 1)
                b = h % 2
                if layer == 1:
                    V.tensor_reduce(negmax[:, b, :], bank2(b, NT), AX, ALU.min).then_inc(s_sc, NT)
                    return
                dve.wait_ge(s_bias, h + 1)
                if h >= 2:
                    dve.wait_ge(s_p, h - 1)
                for t in range(NT):
                    ins = V.tensor_tensor_reduce(score[:, b, t, :], bank2(b, NT)[:, t, :], bias[:, b, t, :],
                                                 1.0, 3.0e38, ALU.add, ALU.min, negmax[:, b, t:t + 1])
                    if h < A_HEADS:
                        ins.then_inc(s_sc, 1)
                    else:
                        link(ins)
                if h >= A_HEADS:
                    k = h - A_HEADS
                    V.tensor_tensor(negmax[:, b, :], negmax[:, b, :], neg_sink[:, k:k + 1].to_broadcast([P, NT]),
                                    ALU.min).then_inc(s_sc, NT)

            def normalise_prob(layer, h):
                g, b = HEADS * layer + h, h % 2
                dve.wait_ge(s_p, g + 1)
                if layer == 0 and h >= A_HEADS:
                    link(V.tensor_tensor(rowsum[:, b, :], rowsum[:, b, :], sink_e[:, b, :], ALU.add))
                link(V.reciprocal(rowinv[:, b, :], rowsum[:, b, :]))
                for t in range(NT):
                    ins = V.tensor_scalar(prob[:, b, t, :], prob[:, b, t, :], rowinv[:, b, t:t + 1], None, ALU.mult)
                ins.then_inc(s_norm, 1)

            def residual(where, done, value):
                dve.wait_ge(done, value)
                for t in range(NT):
                    for half in range(2):
                        xs = x[:, t, half * HALF:(half + 1) * HALF]
                        ins = V.tensor_tensor(xs, bank(where[t][half]), xs, ALU.add)
                        if half == 0:
                            n[0] += 1
                            ins.then_inc(s_dve, 1)
                            dve.wait_ge(s_dve, n[0])
                    ins.then_inc(s_x0, 1)

            def router(layer):
                G = [r_g[:, i, :, :] for i in range(6)]
                E = [r_e[:, i, :, :] for i in range(8)]
                S = [r_s[:, i, :] for i in range(12)]
                rev4 = cst[:, C_REV4:C_REV4 + GROUPS].unsqueeze(1).to_broadcast([P, NT, GROUPS])
                rev32 = cst[:, C_REV32:C_REV32 + EXPERTS].unsqueeze(1).to_broadcast([P, NT, EXPERTS])

                def over(s, k):
                    return s.unsqueeze(2).to_broadcast([P, NT, k])

                dve.wait_ge(s_rl_ps, layer + 1)
                link(V.tensor_tensor(logit[:, :, :], bank(6)[:, 0:NT * NR].rearrange("p (t n) -> p t n", t=NT),
                                     router_b[:, layer, :].unsqueeze(1).to_broadcast([P, NT, NR]), ALU.add))
                lg, le = logit[:, :, 0:GROUPS], logit[:, :, GROUPS:NR]
                link(V.tensor_reduce(S[0], lg, AX, ALU.max))
                V.tensor_tensor(G[4], lg, over(S[0], GROUPS), ALU.subtract).then_inc(s_rd, 1)
                link(V.tensor_tensor(G[0], lg, over(S[0], GROUPS), ALU.is_equal))
                link(V.tensor_tensor(G[1], G[0], rev4, ALU.mult))
                link(V.tensor_reduce(S[1], G[1], AX, ALU.max))
                link(V.tensor_tensor(G[2], G[1], over(S[1], GROUPS), ALU.is_equal))
                link(V.tensor_scalar(G[3], G[2], -1.0, 1.0e37, ALU.add, ALU.mult))
                link(V.tensor_tensor(E[0].rearrange("p t (g e) -> p t g e", g=GROUPS),
                                     le.rearrange("p t (g e) -> p t g e", g=GROUPS),
                                     G[3].unsqueeze(3).to_broadcast([P, NT, GROUPS, PER_GROUP]), ALU.add))

                def best(src, top, onehot):
                    link(V.tensor_reduce(top, src, AX, ALU.max))
                    link(V.tensor_tensor(E[1], src, over(top, EXPERTS), ALU.is_equal))
                    link(V.tensor_tensor(E[2], E[1], rev32, ALU.mult))
                    link(V.tensor_reduce(S[2], E[2], AX, ALU.max))
                    link(V.tensor_tensor(onehot, E[2], over(S[2], EXPERTS), ALU.is_equal))

                best(E[0], S[3], E[3])
                link(V.scalar_tensor_tensor(E[4], E[3], -3.0e37, E[0], ALU.mult, ALU.add))
                best(E[4], S[4], E[5])
                V.tensor_tensor(r_e[:, 7, :, :], E[3], E[5], ALU.add).then_inc(s_pick, 1)
                V.tensor_tensor(S[5], S[4], S[3], ALU.subtract).then_inc(s_rd, 1)
                dve.wait_ge(s_re, 2 * layer + 2)
                link(V.tensor_reduce(S[7], G[5], AX, ALU.add))
                link(V.tensor_scalar(S[8], S[6], 1.0, None, ALU.add))
                link(V.tensor_tensor(S[9], S[8], S[7], ALU.mult))
                link(V.reciprocal(weight[:, 0, :], S[9]))
                link(V.tensor_tensor(weight[:, 1, :], weight[:, 0, :], S[6], ALU.mult))
                base = cst[:, C_BASE:C_BASE + EXPERTS].unsqueeze(1).to_broadcast([P, NT, EXPERTS])
                for i in range(2):
                    link(V.tensor_tensor(E[6], base, E[3 + 2 * i], ALU.mult))
                    link(V.tensor_reduce(first_slot[:, i, :], E[6], AX, ALU.add))
                dve.wait_ge(s_pos_ps, layer + 1)
                pos = bank(0)[:, 0:NT * EXPERTS].rearrange("p (t e) -> p t e", t=NT)
                for i in range(2):
                    link(V.tensor_tensor(E[6], pos, E[3 + 2 * i], ALU.mult))
                    link(V.tensor_reduce(rank[:, i, :], E[6], AX, ALU.add))
                link(V.tensor_reduce(most_f[:, :], bank(1)[0:1, 0:EXPERTS], AX, ALU.max))
                V.tensor_copy(most_i[:, :], most_f[:, :]).then_inc(s_most, 1)

            def experts(rd, rnd):
                sig = rd.sig

                def flat(v):
                    return v.rearrange("p i t -> p (i t)")

                links = [0]

                def then(ins):
                    links[0] += 1
                    ins.then_inc(sig.slots, 1)
                    dve.wait_ge(sig.slots, PER_SLOTS * rounds + links[0])

                rounds = rd.layer if sig is main else (ROUNDS - 1) * rd.layer - 1 + rnd
                if sig is extra:
                    dve.wait_ge(main.chain, 8 * (BATCHES * (rd.layer + 1) + 1))
                if sig is extra or rd.layer:
                    dve.wait_ge(sig.chain, 8 * rd.first)
                if sig is extra:
                    then(V.tensor_scalar(flat(rank[:, :, :]), flat(rank[:, :, :]), -float(SLOTS), None, ALU.add))
                else:
                    then(V.memset(flat(inside[:, 1, :, :]), 0.0))
                lo, both = flat(inside[:, 0, :, :]), flat(inside[:, 1, :, :])
                fr, fs = flat(rank[:, :, :]), flat(slot[:, :, :])
                then(V.tensor_scalar(lo, fr, 0.0, None, ALU.is_ge))
                then(V.scalar_tensor_tensor(both, fr, float(SLOTS), lo, ALU.is_lt, ALU.mult))
                then(V.tensor_scalar(lo, both, -1.0, 1.0e6, ALU.add, ALU.mult))
                then(V.tensor_tensor(fs, fr, flat(first_slot[:, :, :]), ALU.add))
                V.tensor_tensor(fs, fs, lo, ALU.add).then_inc(sig.slots, 1)
                assert links[0] == PER_SLOTS - 1

                def batch(step, place):
                    g = rd.batches_before(step, place)
                    dve.wait_ge(sig.slots, PER_SLOTS * (rounds + 1))
                    dve.wait_ge(sig.chain, 8 * g)
                    dve.wait_ge(sig.gather_ps, 2 * g)
                    dve.wait_ge(sig.added, g)
                    for t in range(NT):
                        V.tensor_scalar(onehot[:, 1, t, :], iota, slot[:, 0, t:t + 1], None, ALU.is_equal)\
                            .then_inc(sig.chain, 1)
                    dve.wait_ge(sig.chain, 8 * g + 2)
                    for t in range(NT):
                        ins = V.scalar_tensor_tensor(onehot[:, 0, t, :], iota, slot[:, 1, t:t + 1], onehot[:, 1, t, :],
                                                     ALU.is_equal, ALU.add)
                    ins.then_inc(sig.onehot, 1)
                    dve.wait_ge(sig.scatter_ps, g)
                    dve.wait_ge(sig.onehot, g + 1)
                    for t in range(NT):
                        V.tensor_scalar(onehot[:, 1, t, :], iota, slot[:, 0, t:t + 1], weight[:, 0, t:t + 1],
                                        ALU.is_equal, ALU.mult).then_inc(sig.chain, 1)
                        V.tensor_scalar(weighted2[:, t, :], iota, slot[:, 1, t:t + 1], weight[:, 1, t:t + 1],
                                        ALU.is_equal, ALU.mult).then_inc(sig.chain, 1)
                    dve.wait_ge(sig.chain, 8 * g + 6)
                    V.tensor_tensor(weighted[:, :, :], onehot[:, 1, :, :], weighted2[:, :, :], ALU.add)\
                        .then_inc(sig.weighted, 1)
                    V.tensor_scalar(fs, fs, -float(P), None, ALU.add).then_inc(sig.chain, 2)
                    for h in range(2):
                        dve.wait_ge(sig.gather_ps, 2 * g + h + 1)
                        V.tensor_tensor(gathered[:, 0, 4 * h:4 * h + 4, :], bank2(4 + h, 4),
                                        gains[:, 2 * rd.layer + 1, 4 * h:4 * h + 4].unsqueeze(2)
                                        .to_broadcast([P, 4, P]), ALU.mult).then_inc(sig.gather, 1)
                    dve.wait_ge(sig.used, rd.units_used(step, place, 1))
                    dve.wait_ge(sig.silu, g + 1)
                    V.tensor_tensor(hidden, bank(1)[:, 0:DFF], silu, ALU.mult).then_inc(sig.hidden, 1)
                    dve.wait_ge(sig.used, rd.units_used(step, place, 2))
                    V.tensor_copy(outputs[:, HALF:D], bank(3)).then_inc(sig.out_v, 1)
                    for half in range(2):
                        for t in range(NT):
                            dve.wait_ge(sig.y_ps, 4 * g + 2 * half + t + 1)
                            xs = x[:, t, half * HALF:(half + 1) * HALF]
                            ins = V.tensor_tensor(xs, bank(Y_MOE[t][half]), xs, ALU.add)
                    ins.then_inc(sig.added, 1)

                over_batches(dve, batch)

            start_signals(dve, main.by_dve, extra.by_dve)
            for layer in range(2):
                normalise(2 * layer)
                take_tokT(2 * layer)
                for s in range(SLABS[layer]):
                    slab(layer, s)
                for h in range(HEADS + 1):
                    if h < HEADS:
                        maxima(layer, h)
                    if h >= 1:
                        normalise_prob(layer, h - 1)
                residual(Y_MIX, s_used, first_unit(layer, "experts"))
                normalise(2 * layer + 1)
                take_tokT(2 * layer + 1)
                router(layer)
                all_rounds(dve, layer, experts, [(extra.slots, PER_SLOTS)] + per_round(extra.by_dve))


_INS = ['x', 'mix_norm', 'ffn_norm', 'ab_w_in', 'a_q_norm', 'a_k_norm', 'b_q_norm', 'b_k_norm', 'b_sink',
        'ab_w_out', 'c_w_in', 'c_q_norm', 'c_k_norm', 'c_w_out', 'moe_group_w', 'moe_group_b', 'moe_expert_w',
        'moe_expert_b', 'moe_w_gate', 'moe_w_up', 'moe_w_down']


def kernel(**inputs):
    import concourse.bacc as bacc
    from concourse.bass_utils import run_bass_kernel_spmd

    nc = bacc.Bacc("TRN2", target_bir_lowering=False, num_devices=1)
    arrays, args = {}, []
    for name in _INS + ["shape_constants"]:
        a = shape_constants() if name == "shape_constants" else np.ascontiguousarray(inputs[name])
        arrays[f"in_{name}"] = a
        args.append(nc.dram_tensor(f"in_{name}", a.shape, F32, kind="ExternalInput").ap())
    out = nc.dram_tensor("out_x", (1, SEQ, D), F32, kind="ExternalOutput").ap()
    hybrid_moe_kernel(nc, *args, out)
    r = run_bass_kernel_spmd(nc, [arrays], core_ids=[0])
    return r.results[0]["out_x"]
```

```python
from contextlib import ExitStack

import numpy as np
import concourse.bass as bass
from concourse import mybir

ALU = mybir.AluOpType
ACT = mybir.ActivationFunctionType
F32 = mybir.dt.float32
I32 = mybir.dt.int32
AX = mybir.AxisListType.X

P = 128
D = 1024
SEQ = 256
NT = SEQ // P
NC = D // P
HD = 64
HEADS = 16
A_HEADS = B_HEADS = 8
GRID_W = 64
EPS = 1e-6
GROUPS, PER_GROUP = 4, 8
EXPERTS = GROUPS * PER_GROUP
DFF = 256
NR = GROUPS + EXPERTS
SLOTS = 32
ROUNDS = SEQ // SLOTS
BATCH = 4
BATCHES = EXPERTS // BATCH
HALF = 512
FAR = 1e30
UNIT = 2048
RING = 16
STAGE = BATCH
PER_BATCH = 3 * STAGE
PER_ROUND = 3 * EXPERTS
LOOP = 4
SLABS = (9, 6)
OUTS = 4

C_IDENT = 0
C_TRI = C_IDENT + P
C_ONES = C_TRI + P
C_IOTA = C_ONES + P
C_REV4 = C_IOTA + P
C_REV32 = C_REV4 + GROUPS
C_BASE = C_REV32 + EXPERTS
C_DIST = C_BASE + EXPERTS
C_MA = C_DIST + NT * SEQ
C_MB = C_MA + NT * SEQ
C_KEEP = C_MB + NT * SEQ
C_COS = C_KEEP
C_SIN = C_COS + NT * HD
C_ALL = C_SIN + NT * HD


def shape_constants():
    t = np.zeros((P, C_ALL), np.float32)
    t[:, C_IDENT:C_IDENT + P] = np.eye(P)
    t[:, C_TRI:C_TRI + P] = np.triu(np.ones((P, P)), 1)
    t[:, C_ONES:C_ONES + P] = 1.0
    t[:, C_IOTA:C_IOTA + P] = np.arange(P)[None]
    q = (np.arange(NT)[None, :, None] * P + np.arange(P)[:, None, None])
    k = np.arange(SEQ)[None, None, :]
    dist = np.abs(q - k)
    t[:, C_DIST:C_DIST + NT * SEQ] = dist.reshape(P, -1)
    count = (dist <= 64).astype(int)
    for window, dil in ((512, 4), (2048, 16)):
        count = count + ((dist % dil == 0) & (dist <= window // 2))
    t[:, C_MA:C_MA + NT * SEQ] = np.where(count > 0, -np.log(np.maximum(count, 1)), FAR).reshape(P, -1)
    t[:, C_MB:C_MB + NT * SEQ] = np.where(dist <= 128, 0.0, FAR).reshape(P, -1)
    inv_freq = np.float32(10000.0) ** (-np.arange(0, 32, 2, dtype=np.float32) / np.float32(32))
    tok = q[:, :, 0]
    cos, sin = [], []
    for axis in ((tok // GRID_W), (tok % GRID_W)):
        ang = (axis.astype(np.float32)[..., None] * inv_freq).astype(np.float32)
        cos += [np.cos(ang), np.cos(ang)]
        sin += [-np.sin(ang), np.sin(ang)]
    t[:, C_COS:C_COS + NT * HD] = np.concatenate(cos, -1).reshape(P, -1)
    t[:, C_SIN:C_SIN + NT * HD] = np.concatenate(sin, -1).reshape(P, -1)
    t[:, C_REV4:C_REV4 + GROUPS] = np.arange(GROUPS, 0, -1)[None]
    t[:, C_REV32:C_REV32 + EXPERTS] = np.arange(EXPERTS, 0, -1)[None]
    t[:, C_BASE:C_BASE + EXPERTS] = SLOTS * np.arange(EXPERTS)[None]
    return t


def slope(i):
    return float(np.float32(2.0 ** (-8.0 * (i + 1) / HEADS)))


def first_unit(layer, part):
    at = 0 if layer == 0 else SLABS[0] + OUTS + PER_ROUND
    return at + {"in": 0, "out": SLABS[layer], "experts": SLABS[layer] + OUTS}[part]


def hybrid_moe_kernel(nc, x_d, mix_norm, ffn_norm, ab_w_in, a_q_norm, a_k_norm, b_q_norm, b_k_norm, b_sink,
                      ab_w_out, c_w_in, c_q_norm, c_k_norm, c_w_out, moe_group_w, moe_group_b, moe_expert_w,
                      moe_expert_b, moe_w_gate, moe_w_up, moe_w_down, cst_d, out_d):
    with ExitStack() as ctx:
        def sb(name, shape, dt=F32):
            return ctx.enter_context(nc.sbuf_tensor(name, shape, dt))

        def sem(name):
            return ctx.enter_context(nc.semaphore(name))

        ring = [sb(f"ring{i}", [P, UNIT]) for i in range(RING)]
        x = sb("x", [P, NT, D])
        tokens = sb("tokens", [P, NT, NC, P])
        tokT = sb("tokT", [P, NC, SEQ])
        cst = sb("cst", [P, C_KEEP])
        area = sb("area", [P, 20 * SEQ + NT * 640 + 2 * HALF])
        work = sb("work", [P, 6 * HALF])
        router_w = sb("router_w", [P, 2, NC, NR])
        router_b = sb("router_b", [P, 2, NR])
        gains = sb("gains", [P, 4, NC])
        head_g = sb("head_g", [P, 4])
        gq_bc = sb("gq_bc", [P, HD])
        gk_bc = sb("gk_bc", [P, HD])
        rope = sb("rope", [P, 4, NT, HD])
        sink = sb("sink", [P, B_HEADS])
        neg_sink = sb("neg_sink", [P, B_HEADS])
        sumsq = sb("sumsq", [P, NT])
        mean = sb("mean", [P, NT])
        rstd = sb("rstd", [P, NT])
        head_eps = sb("head_eps", [P, NT])
        newton = sb("newton", [P, 2, NT * 4])
        head_ss = sb("head_ss", [P, NT * 4])
        head_rs = sb("head_rs", [P, NT * 4])
        negmax = sb("negmax", [P, 2, NT])
        rowsum = sb("rowsum", [P, 2, NT])
        rowinv = sb("rowinv", [P, 2, NT])
        sink_e = sb("sink_e", [P, 2, NT])
        logit = sb("logit", [P, NT, NR])
        r_g = sb("r_g", [P, 6, NT, GROUPS])
        r_s = sb("r_s", [P, 12, NT])
        rank = sb("rank", [P, 2, NT])
        first_slot = sb("first_slot", [P, 2, NT])
        slot = sb("slot", [P, 2, NT])
        inside = sb("inside", [P, 2, 2, NT])
        weight = sb("weight", [P, 2, NT])
        most_i = sb("most_i", [1, 1], I32)
        most_f = sb("most_f", [1, 1])
        banks = ctx.enter_context(nc.psum_tensor("banks", [P, 8, HALF], F32))

        HT_TILES = 20
        headsT = area[:, 0:HT_TILES * SEQ].rearrange("p (n t) -> p n t", t=SEQ)
        KEYS = 8
        VW = 640
        v0 = HT_TILES * SEQ
        values = area[:, v0:v0 + NT * VW].rearrange("p (t n) -> p t n", t=NT)
        bias = area[:, v0 + NT * VW:v0 + NT * VW + 2 * HALF].rearrange("p (b t k) -> p b t k", b=2, t=NT)
        early = work[:, 2 * HALF:4 * HALF]
        raw_gw = early[:, 0:2 * NC * GROUPS].rearrange("p (l n) -> p l n", l=2)
        raw_ew = early[:, 64:64 + 2 * NC * EXPERTS].rearrange("p (l g n) -> p l g n", l=2, g=GROUPS)
        raw_rope = early[:, 576:576 + 2 * NT * HD]
        gathered = area[:, 0:2 * NC * P].rearrange("p (b c s) -> p b c s", b=2, c=NC)
        outputs = area[:, 2048:2048 + D]
        onehot = area[:, 3072:3072 + 2 * NT * P].rearrange("p (b t s) -> p b t s", b=2, t=NT)
        weighted = area[:, 3584:3584 + NT * P].rearrange("p (t s) -> p t s", t=NT)
        weighted2 = area[:, 3840:3840 + NT * P].rearrange("p (t s) -> p t s", t=NT)
        scatter = area[:, 4096:4096 + NT * P]
        silu = area[:, 4352:4352 + DFF]
        hidden = area[:, 4608:4608 + DFF]
        hiddenT = area[:, 4864:4864 + 2 * P].rearrange("p (k s) -> p k s", k=2)
        r_e = area[:, 5120:5120 + 8 * NT * EXPERTS].rearrange("p (i t e) -> p i t e", i=8, t=NT)

        def work3(i):
            return work[:, 2 * i * HALF:2 * (i + 1) * HALF]

        spare = tokens[:, :, :, :].rearrange("p t c k -> p (t c k)")
        square = spare[:, 0:2 * HALF].rearrange("p (b n) -> p b n", b=2)
        normed = spare[:, 2 * HALF:4 * HALF].rearrange("p (b n) -> p b n", b=2)
        rot = work3(1).rearrange("p (b n) -> p b n", b=2)
        prob = work3(0).rearrange("p (b t k) -> p b t k", b=2, t=NT)
        score = work3(1).rearrange("p (b t k) -> p b t k", b=2, t=NT)
        probT = work3(2).rearrange("p (b c q) -> p b c q", b=2, c=NT)
        attT = headsT
        ident = cst[:, C_IDENT:C_IDENT + P]
        tri = cst[:, C_TRI:C_TRI + P]
        ones = cst[:, C_ONES:C_ONES + P]
        iota = cst[:, C_IOTA:C_IOTA + P]

        def bank(i):
            return banks[:, i, :]

        def bank2(i, a):
            return banks[:, i, :].rearrange("p (a b) -> p a b", a=a)

        Y_MIX = [[6, 7], [0, 1]]
        Y_MOE = [[4, 5], [6, 7]]

        s_x = sem("x_loaded")
        s_first = sem("first_constants_loaded")
        s_small = sem("small_inputs_loaded")
        s_unit = [sem(f"unit_loaded{i}") for i in range(RING)]
        s_used = sem("units_used")
        s_prep = sem("pool_prepared")
        s_pchain = sem("pool_chain")
        s_bias = sem("bias_ready")
        s_dve = sem("dve_chain")
        s_x0 = sem("x_updated")
        s_sq = sem("act_square_sum")
        s_rstd = sem("inverse_rms_ready")
        s_tok = sem("tokens_normalised")
        s_proj = sem("mixer_output_in_psum")
        s_count_ps = sem("counts_in_psum")
        s_tokT_ps = sem("tokT_in_psum")
        s_tokT_a = sem("tokT_by_act")
        s_tokT_v = sem("tokT_by_dve")
        s_sqh = sem("head_squares")
        s_slab = sem("slab_taken")
        s_val = sem("values_taken")
        s_hT_ps = sem("headT_in_psum")
        s_hT = sem("headT_ready")
        s_sc_ps = sem("scores_in_psum")
        s_sc = sem("scores_max_ready")
        s_p = sem("prob_ready")
        s_pT_ps = sem("probT_in_psum")
        s_pT = sem("probT_ready")
        s_norm = sem("prob_normalised")
        s_pv_ps = sem("attT_in_psum")
        s_att = sem("attT_ready")
        s_rl_ps = sem("router_logits")
        s_rd = sem("router_differences")
        s_re = sem("router_exponentials")
        s_pick = sem("experts_picked")
        s_pos_ps = sem("ranks_in_psum")
        s_most = sem("largest_count_ready")
        s_zero = sem("keys_cleared")

        class Signals:

            def __init__(self, name):
                self.unit = s_unit if name == "main" else [sem(f"extra_unit{i}") for i in range(RING)]
                self.used = s_used if name == "main" else sem("extra_units_used")
                self.slots = sem(name + "_slots_ready")
                self.chain = sem(name + "_batch_chain")
                self.onehot = sem(name + "_onehot_ready")
                self.weighted = sem(name + "_weighted_ready")
                self.gather_ps = sem(name + "_gathered_in_psum")
                self.gather = sem(name + "_gathered_ready")
                self.scatter_ps = sem(name + "_scatter_in_psum")
                self.scatter = sem(name + "_scatter_ready")
                self.silu = sem(name + "_silu_ready")
                self.hidden = sem(name + "_hidden_ready")
                self.hiddenT_ps = sem(name + "_hiddenT_in_psum")
                self.hiddenT = sem(name + "_hiddenT_ready")
                self.out_ps = sem(name + "_first_half_in_psum")
                self.out_a = sem(name + "_outputs_by_act")
                self.out_v = sem(name + "_outputs_by_dve")
                self.y_ps = sem(name + "_sums_in_psum")
                self.added = sem(name + "_sums_added")
                self.by_pe = [(self.gather_ps, 2), (self.scatter_ps, 1), (self.hiddenT_ps, 1), (self.out_ps, 1),
                              (self.y_ps, 2 * NT)]
                self.by_act = [(self.scatter, 1), (self.silu, 1), (self.hiddenT, 1), (self.out_a, 1)]
                self.by_dve = [(self.chain, 8), (self.onehot, 1), (self.weighted, 1), (self.gather, 2),
                               (self.hidden, 1), (self.out_v, 1), (self.added, 1)]

        main, extra = Signals("main"), Signals("extra")
        s_done = sem("output_stored")

        def loaded(n):
            return 16 * (n // RING + 1)

        class Round:

            def __init__(self, sig, layer, first_batch, unit0, turns):
                self.sig, self.layer, self.first = sig, layer, first_batch
                self.unit0, self.turns = unit0, turns

            def batches_before(self, step, place):
                return self.first + (LOOP * step + place)

            def ring_slot(self, place, stage, j):
                return (self.unit0 + PER_BATCH * place + STAGE * stage + j) % RING

            def unit_loaded(self, step, place, stage, j):
                k = self.unit0 + PER_BATCH * place + STAGE * stage + j
                return 16 * (k // RING + 1) + 16 * (LOOP * PER_BATCH // RING) * step + 16 * self.turns

            def units_used(self, step, place, stage):
                return (self.unit0 + PER_BATCH * place + STAGE * (stage + 1)) + LOOP * PER_BATCH * step \
                    + RING * self.turns

        PER_SLOTS = 6

        def residual_ready(eng, m, t):
            if m == 0:
                eng.wait_ge(s_x, 16 * NT)
            elif m % 2:
                eng.wait_ge(s_x0, NT * (m // 2) + t + 1)
            else:
                eng.wait_ge(main.added, BATCHES * m // 2 + 1)
                eng.wait_ge(extra.added, (ROUNDS - 1) * BATCHES * m // 2 + 1)

        def over_batches(eng, body):
            with eng.Fori(0, BATCHES // LOOP) as step:
                for place in range(LOOP):
                    body(step, place)

        def start_signals(eng, *signals):
            for per_batch in signals:
                for s, count in per_batch:
                    eng.sem_inc(s, count)

        def all_rounds(eng, layer, one_round, counts, after=None):
            one_round(Round(main, layer, BATCHES * layer + 1, first_unit(layer, "experts"), 0), 0)
            eng.wait_ge(s_most, layer + 1)
            most = eng.value_load(most_i[0:1, 0:1], min_val=0, max_val=SEQ)
            with eng.If(most > SLOTS):
                with eng.Fori(1, ROUNDS) as rnd:
                    before = (ROUNDS - 1) * layer - 1 + rnd
                    one_round(Round(extra, layer, before * BATCHES + 1, 0, before * (PER_ROUND // RING) + 1), rnd)
                if after:
                    after()
            with eng.Else():
                for s, count in counts:
                    eng.sem_inc(s, (ROUNDS - 1) * count)

        def per_round(per_batch):
            return [(s, BATCHES * count) for s, count in per_batch]

        def head_place(layer, h):
            if layer == 1:
                return h // 2, KEYS + 2 * (h // 4) + h % 2, HD * (h // 4)
            if h < A_HEADS:
                return h // 2, KEYS + h, HD * h
            return h // 2, KEYS + A_HEADS + 2 * ((h - 8) // 4) + h % 2, 512 + HD * ((h - 8) // 4)

        SLAB_PLAN = [
            [("heads", 0, 0, 0), ("keys", 2, KEYS, 1), ("values", 4, 0, None),
             ("heads", 1, 2, 0), ("keys", 3, KEYS + 4, 1), ("values", 5, 256, None),
             ("heads", 6, 4, 2), ("shared2", 8, KEYS + 8, 3), ("heads", 7, 6, 2)],
            [("shared4", 4, KEYS, "k"), ("values", 5, 0, None),
             ("heads", 0, 0, "q"), ("heads", 1, 2, "q"), ("heads", 2, 4, "q"), ("heads", 3, 6, "q")],
        ]
        QK_SLAB = [[1, 4, 7, 8], [2, 3, 4, 5]]
        V_SLAB = [[2, 5, 7, 7], [1, 1, 1, 1]]
        EARLY = (3, 4)
        PARTS = 4
        PARTS_AT = [[3] * 8, [1] * 8]
        OUT_AT = {9: (0, 0), 10: (0, 1), 11: (1, 0), 12: (1, 1), 15: (2, 0), 16: (2, 1)}

        def mixer_order(layer):
            parts = [(s, part) for s in range(SLABS[layer]) for part in range(PARTS)]
            order = []

            def fill(count):
                for _ in range(count):
                    s, part = parts.pop(0)
                    order.append(("slab", s, part))
                    if part == 0 and s:
                        order.append(("rotate", s - 1, 0))
                    if part == 2 and s:
                        order.append(("turn_heads", s - 1, 0))

            fill(EARLY[layer] * PARTS)
            for h in range(HEADS + 2):
                if h < HEADS:
                    order.append(("scores", h, 0))
                if h < len(PARTS_AT[layer]):
                    fill(PARTS_AT[layer][h])
                if h == len(PARTS_AT[layer]):
                    order.append(("rotate", SLABS[layer] - 1, 0))
                if h == len(PARTS_AT[layer]) + 1:
                    order.append(("turn_heads", SLABS[layer] - 1, 0))
                if h in OUT_AT:
                    order.append(("project_out",) + OUT_AT[h])
                if h >= 3 and h % 2 == 1:
                    order.append(("prob_values", (h - 3) // 2, 0))
                if 1 <= h <= HEADS:
                    order.append(("turn_prob", h - 1, 0))
            assert not parts
            return order

        TURNS = [[], []]
        for lay in range(2):
            for s, (kind, _, tile, g) in enumerate(SLAB_PLAN[lay]):
                if kind in ("heads", "keys", "shared2"):
                    TURNS[lay].append((s, tile, g, 0))
                elif kind == "shared4":
                    TURNS[lay] += [(s, tile, g, 0), (s, tile + 4, g, 1)]

        def turns_before(layer, slab):
            return (len(TURNS[0]) if layer else 0) + sum(t[0] < slab for t in TURNS[layer])

        def norm_slabs_before(layer, slab):
            n = sum(k != "values" for k, *_ in SLAB_PLAN[0]) if layer else 0
            return n + sum(k != "values" for k, *_ in SLAB_PLAN[layer][:slab])

        NORMED = [(lay, s) for lay in range(2) for s in range(SLABS[lay]) if SLAB_PLAN[lay][s][0] != "values"]

        def values_before(layer, slab):
            n = sum(k in ("values", "shared2") for k, *_ in SLAB_PLAN[0]) if layer else 0
            return n + sum(k in ("values", "shared2") for k, *_ in SLAB_PLAN[layer][:slab])

        def head_rows(layer, s, k, part):
            if SLAB_PLAN[layer][s][0] == "shared4":
                return normed[:, part, :].rearrange("p (t n) -> p t n", t=NT)
            return normed[:, k, :].rearrange("p (t n) -> p t n", t=NT)

        block = ctx.enter_context(nc.Block())

        @block.sync
        def _(sp):
            for u in extra.unit:
                sp.sem_inc(u, 16)
            for t in range(NT):
                sp.dma_start(x[:, t, :], x_d[0, t * P:(t + 1) * P, :]).then_inc(s_x, 16)
            sp.dma_start(cst[:, C_IDENT:C_IDENT + P], cst_d[:, C_IDENT:C_IDENT + P]).then_inc(s_first, 16)
            for m in range(2):
                sp.dma_start(gains[:, m:4:2, :], (mix_norm, ffn_norm)[m].rearrange("l (p c) -> p l c", c=NC))\
                    .then_inc(s_first, 16)

            def room(n):
                if n >= RING:
                    sp.wait_ge(s_used, n - RING + 1)

            def load_in(layer, s):
                w_in = (ab_w_in, c_w_in)[layer][0].rearrange("(p c) n -> p c n", c=NC)
                n, col = first_unit(layer, "in") + s, SLAB_PLAN[layer][s][1]
                room(n)
                sp.dma_start(ring[n % RING][:, :].rearrange("p (c n) -> p c n", c=NC),
                             w_in[:, :, 256 * col:256 * col + 256]).then_inc(s_unit[n % RING], 16)

            def load_small():
                sp.dma_start(cst[:, P:C_KEEP], cst_d[:, P:C_KEEP]).then_inc(s_small, 16)
                sp.dma_start(raw_rope, cst_d[:, C_KEEP:C_ALL]).then_inc(s_small, 16)
                for c, g in enumerate((a_q_norm, a_k_norm, b_q_norm, b_k_norm)):
                    for r in range(2):
                        sp.dma_start(head_g[r * HD:(r + 1) * HD, c:c + 1], g[0].rearrange("(p c) -> p c", c=1))\
                            .then_inc(s_small, 16)
                sp.dma_start(gq_bc[:, :], c_q_norm[0].partition_broadcast(P)).then_inc(s_small, 16)
                sp.dma_start(gk_bc[:, :], c_k_norm[0].partition_broadcast(P)).then_inc(s_small, 16)
                sp.dma_start(sink[:, :], b_sink[0].partition_broadcast(P)).then_inc(s_small, 16)
                sp.dma_start(raw_gw, moe_group_w.rearrange("l (p c) g -> p l (c g)", c=NC)).then_inc(s_small, 16)
                for l in range(2):
                    sp.dma_start(raw_ew[:, l, :, :], moe_expert_w[l].rearrange("g (p c) e -> p g (c e)", c=NC))\
                        .then_inc(s_small, 16)
                    sp.dma_start(router_b[:, l, 0:GROUPS], moe_group_b[l].partition_broadcast(P)).then_inc(s_small, 16)
                    sp.dma_start(router_b[:, l, GROUPS:NR],
                                 moe_expert_b[l].rearrange("g e -> (g e)").partition_broadcast(P)).then_inc(s_small, 16)

            for layer in range(2):
                for s in range(SLABS[layer]):
                    load_in(layer, s)
                    if layer == 0 and s == 1:
                        load_small()
                w_out = (ab_w_out, c_w_out)[layer][0]
                for s in range(OUTS):
                    n = first_unit(layer, "out") + s
                    room(n)
                    sp.dma_start(ring[n % RING][:, :].rearrange("p (c n) -> p c n", c=2),
                                 w_out[256 * s:256 * s + 256, :].rearrange("(c p) n -> p c n", p=P))\
                        .then_inc(s_unit[n % RING], 16)
                gate = moe_w_gate[layer].rearrange("g e (p c) f -> (g e) p (c f)", c=NC)
                up = moe_w_up[layer].rearrange("g e (p c) f -> (g e) p (c f)", c=NC)
                down = moe_w_down[layer].rearrange("g e (c p) n -> (g e) p c n", p=P)

                def load_round(rd, rnd):
                    sig = rd.sig
                    if sig is extra:
                        sp.wait_ge(s_used, first_unit(layer, "experts") + PER_ROUND)
                        sp.wait_ge(sig.used, RING * rd.turns)
                    for b in range(BATCHES):
                        for stage, w in enumerate((gate, up, down)):
                            for j in range(STAGE):
                                k = rd.unit0 + PER_BATCH * b + STAGE * stage + j
                                if k >= RING:
                                    sp.wait_ge(sig.used, RING * rd.turns + k - RING + 1)
                                e = BATCH * b + j
                                if stage < 2:
                                    src, dst = w[e], ring[k % RING][:, :]
                                else:
                                    src, dst = w[e], ring[k % RING][:, :].rearrange("p (c n) -> p c n", c=2)
                                sp.dma_start(dst, src).then_inc(sig.unit[k % RING], 16)

                def last_used():
                    sp.wait_ge(extra.used, (ROUNDS - 1) * PER_ROUND * (layer + 1) + RING)

                all_rounds(sp, layer, load_round, [(u, 16 * PER_ROUND // RING) for u in extra.unit], last_used)
            sp.wait_ge(main.added, 2 * BATCHES + 1)
            sp.wait_ge(extra.added, 2 * (ROUNDS - 1) * BATCHES + 1)
            for t in range(NT):
                sp.dma_start(out_d[0, t * P:(t + 1) * P, :], x[:, t, :]).then_inc(s_done, 16)
            sp.wait_ge(s_done, 16 * NT)

        SMALL = 2 + 8 + 3 + 1 + 2 * 3

        @block.gpsimd
        def _(pool):
            n = [0]

            def link(ins):
                n[0] += 1
                ins.then_inc(s_pchain, 1)
                pool.wait_ge(s_pchain, n[0])

            pool.wait_ge(s_first, 48)
            pool.wait_ge(s_small, 16 * SMALL)
            for c in (0, 2):
                link(nc.gpsimd.tensor_scalar(head_g[:, c:c + 1], head_g[:, c:c + 1], -1.0, None, ALU.mult))
            for c in (1, 3):
                link(nc.gpsimd.tensor_scalar(head_g[:, c:c + 1], head_g[:, c:c + 1], 8.0, None, ALU.mult))
            nc.gpsimd.tensor_scalar(neg_sink[:, :], sink[:, :], -1.0, None, ALU.mult).then_inc(s_prep, 1)

            def table(h):
                if h >= 2:
                    pool.wait_ge(s_sc, 2 * (h - 1))
                mask = (C_MA, C_MB)[h // A_HEADS]
                i = 2 * h if h < A_HEADS else 2 * (h - A_HEADS) + 1
                b = bias[:, h % 2, :, :].rearrange("p t k -> p (t k)")
                link(nc.gpsimd.tensor_scalar(b, cst[:, C_DIST:C_DIST + HALF], slope(i), None, ALU.mult))
                nc.gpsimd.tensor_tensor(b, b, cst[:, mask:mask + HALF], ALU.add).then_inc(s_bias, 1)

            keys = area[:, KEYS * SEQ:HT_TILES * SEQ]
            nc.gpsimd.memset(keys, 0.0).then_inc(s_zero, 1)
            for layer in range(2):
                nc.gpsimd.tensor_copy(router_w[:, layer, :, 0:GROUPS],
                                      raw_gw[:, layer, :].rearrange("p (c g) -> p c g", c=NC)).then_inc(s_prep, 1)
                for g in range(GROUPS):
                    a = GROUPS + g * PER_GROUP
                    nc.gpsimd.tensor_copy(router_w[:, layer, :, a:a + PER_GROUP],
                                          raw_ew[:, layer, g, :].rearrange("p (c e) -> p c e", c=NC))\
                        .then_inc(s_prep, 1)
            for i, (g, scale) in enumerate(((gq_bc, -1.0), (gk_bc, 8.0))):
                link(nc.gpsimd.tensor_scalar(g[:, :], g[:, :], scale, None, ALU.mult))
                for t in range(NT):
                    nc.gpsimd.tensor_tensor(rope[:, 2 * i, t, :], raw_rope[:, HD * t:HD * t + HD],
                                            g[:, :], ALU.mult).then_inc(s_prep, 1)
                    for b in range(2):
                        sin_v = raw_rope[:, HD * (NT + t):HD * (NT + t + 1)].rearrange("p (a b j) -> p a b j", a=2, b=2)
                        nc.gpsimd.tensor_tensor(
                            rope[:, 2 * i + 1, t, :].rearrange("p (a b j) -> p a b j", a=2, b=2)[:, :, b, :],
                            sin_v[:, :, b, :],
                            g[:, :].rearrange("p (a b j) -> p a b j", a=2, b=2)[:, :, 1 - b, :],
                            ALU.mult).then_inc(s_prep, 1)
            for h in range(HEADS):
                table(h)
            pool.wait_ge(s_tokT_ps, 4 * 2 + 1)
            nc.gpsimd.memset(keys, 0.0).then_inc(s_zero, 1)

        PREP = 1 + 2 * (1 + GROUPS) + 2 * NT * 3

        @block.tensor
        def _(pe):
            def transpose_tokens(m, t):
                residual_ready(pe, m, t)
                if m == 0:
                    pe.wait_ge(s_first, 48)
                rows = x[:, t, :].rearrange("q (p c) -> q c p", c=NC)
                for c in range(NC):
                    ins = pe.transpose(bank(2 + 2 * t + c // 4)[:, c % 4 * P:(c % 4 + 1) * P], rows[:, c, :], ident)
                    if c % 4 == 3:
                        ins.then_inc(s_tokT_ps, 1)

            def tokT_ready(m, t):
                pe.wait_ge(s_tokT_a, NT * m + t + 1)
                pe.wait_ge(s_tokT_v, NT * m + t + 1)

            def slab(layer, s, part):
                n = first_unit(layer, "in") + s
                if s >= 2 and part == 0:
                    pe.wait_ge(s_slab, norm_slabs_before(layer, s - 1))
                    pe.wait_ge(s_val, values_before(layer, s - 1))
                pe.wait_ge(s_unit[n % RING], loaded(n))
                w = ring[n % RING][:, :].rearrange("p (c n) -> p c n", c=NC)
                t = part // 2
                if s == 0 and part % 2 == 0:
                    tokT_ready(2 * layer, t)
                for c in range(NC // 2 * (part % 2), NC // 2 * (part % 2 + 1)):
                    ins = pe.matmul(bank2(6 + s % 2, NT)[:, t, :], tokT[:, c, t * P:(t + 1) * P], w[:, c, :],
                                    start=(c == 0), stop=(c == NC - 1))
                if part == PARTS - 1:
                    ins.then_inc(s_used, 1)

            def turn_heads(layer, s):
                done = turns_before(layer, s)
                for (ts, tile, g, part) in TURNS[layer]:
                    if ts != s:
                        continue
                    pe.wait_ge(s_slab, norm_slabs_before(layer, s) + 1)
                    if done:
                        pe.wait_ge(s_hT, done)
                    k = norm_slabs_before(layer, s) % 2
                    for c in range(2):
                        for t in range(NT):
                            src = head_rows(layer, s, k, part)[:, t, c * P:(c + 1) * P]
                            ins = pe.transpose(bank2(5, 2)[:, c, t * P:(t + 1) * P], src, ident)
                    ins.then_inc(s_hT_ps, 1)
                    done += 1

            def scores(layer, h):
                g = HEADS * layer + h
                qt, kt, _ = head_place(layer, h)
                if h % 4 == 0:
                    pe.wait_ge(s_hT, turns_before(layer, QK_SLAB[layer][h // 4] + 1))
                if h >= 2:
                    if layer == 0:
                        pe.wait_ge(s_sc, NT * (g - 1))
                    else:
                        pe.wait_ge(s_p, g - 1)
                for t in range(NT):
                    ins = pe.matmul(bank2(h % 2, NT)[:, t, :], headsT[:, qt, t * P:(t + 1) * P],
                                    headsT[:, kt, :], start=True, stop=True)
                ins.then_inc(s_sc_ps, 1)

            def turn_prob(layer, h):
                g = HEADS * layer + h
                pe.wait_ge(s_norm, g + 1)
                if h >= 2:
                    pe.wait_ge(s_pT, g - 1)
                for c in range(NT):
                    for t in range(NT):
                        ins = pe.transpose(bank2(2 + h % 2, NT)[:, c, t * P:(t + 1) * P],
                                           prob[:, h % 2, t, c * P:(c + 1) * P], ident)
                ins.then_inc(s_pT_ps, 1)

            def prob_values(layer, i):
                pe.wait_ge(s_pT, HEADS * layer + 2 * i + 2)
                pe.wait_ge(s_val, values_before(layer, V_SLAB[layer][i // 2] + 1))
                if i:
                    pe.wait_ge(s_att, HEADS // 2 * layer + i)
                for c in range(NT):
                    for r in range(2):
                        vcol = head_place(layer, 2 * i + r)[2]
                        ins = pe.matmul(bank(4)[r * HD:(r + 1) * HD, 0:SEQ], values[:, c, vcol:vcol + HD],
                                        probT[:, r, c, :], start=(c == 0), stop=(c == NT - 1))
                ins.then_inc(s_pv_ps, 1)

            def project_out(layer, u, t, half):
                n = first_unit(layer, "out") + u
                if (u, t, half) == (0, 0, 0):
                    pe.wait_ge(s_slab, norm_slabs_before(layer, SLABS[layer]))
                    pe.wait_ge(s_val, values_before(layer, SLABS[layer]))
                pe.wait_ge(s_att, HEADS // 2 * layer + 2 * u + 2)
                pe.wait_ge(s_unit[n % RING], loaded(n))
                w = ring[n % RING][:, :].rearrange("p (c n) -> p c n", c=2)
                for c in range(2):
                    k = 2 * u + c
                    ins = pe.matmul(bank(Y_MIX[t][half]), attT[:, k, t * P:(t + 1) * P],
                                    w[:, c, half * HALF:(half + 1) * HALF],
                                    start=(k == 0), stop=(k == NC - 1))
                if t == 1 and half == 1:
                    ins.then_inc(s_used, 1)
                elif u == OUTS - 1 and (t, half) != (0, 0):
                    ins.then_inc(s_proj, 1)

            def router_logits(layer, t):
                tokT_ready(2 * layer + 1, t)
                if layer == 0:
                    pe.wait_ge(s_prep, PREP)
                for c in range(NC):
                    ins = pe.matmul(bank(6)[:, t * NR:(t + 1) * NR], tokT[:, c, t * P:(t + 1) * P],
                                    router_w[:, layer, c, :], start=(c == 0), stop=(c == NC - 1))
                ins.then_inc(s_rl_ps, 1)

            def ranks(layer):
                pe.wait_ge(s_pick, layer + 1)
                picked = r_e[:, 7, :, :]
                for t in range(NT):
                    o = bank(0)[:, t * EXPERTS:(t + 1) * EXPERTS]
                    for b in range(t):
                        pe.matmul(o, ones, picked[:, b, :], start=(b == 0), stop=False)
                    ins = pe.matmul(o, tri, picked[:, t, :], start=(t == 0), stop=True)
                ins.then_inc(s_pos_ps, 1)
                for t in range(NT):
                    ins = pe.matmul(bank(1)[:, 0:EXPERTS], ones, picked[:, t, :], start=(t == 0), stop=(t == NT - 1))
                ins.then_inc(s_count_ps, 1)

            def experts(rd, rnd):
                sig, layer = rd.sig, rd.layer
                if sig is extra:
                    pe.wait_ge(main.added, BATCHES * (layer + 1) + 1)
                else:
                    pe.wait_ge(s_tok, NT * (layer + 1))

                def batch(step, place):
                    g = rd.batches_before(step, place)

                    def arrived(stage):
                        for j in range(STAGE):
                            pe.wait_ge(sig.unit[rd.ring_slot(place, stage, j)], rd.unit_loaded(step, place, stage, j))

                    pe.wait_ge(sig.onehot, g + 1)
                    pe.wait_ge(sig.added, g)
                    for c in range(NC):
                        for t in range(NT):
                            ins = pe.matmul(bank(4 + c // 4)[:, c % 4 * P:(c % 4 + 1) * P], tokens[:, t, c, :],
                                            onehot[:, 0, t, :], start=(t == 0), stop=(t == NT - 1))
                        if c % 4 == 3:
                            ins.then_inc(sig.gather_ps, 1)
                    pe.wait_ge(sig.weighted, g + 1)
                    for t in range(NT):
                        ins = pe.transpose(bank(7)[:, t * P:(t + 1) * P], weighted[:, t, :], ident)
                    ins.then_inc(sig.scatter_ps, 1)
                    pe.wait_ge(sig.gather, 2 * (g + 1))
                    pe.wait_ge(s_most, layer + 1)
                    pe.wait_ge(sig.hidden, g)
                    for stage in range(2):
                        arrived(stage)
                        for c in range(NC):
                            for j in range(BATCH):
                                w = ring[rd.ring_slot(place, stage, j)][:, :].rearrange("p (c n) -> p c n", c=NC)
                                ins = pe.matmul(bank(stage)[j * SLOTS:(j + 1) * SLOTS, 0:DFF],
                                                gathered[:, 0, c, j * SLOTS:(j + 1) * SLOTS], w[:, c, :],
                                                start=(c == 0), stop=(c == NC - 1))
                        ins.then_inc(sig.used, STAGE)
                    pe.wait_ge(sig.hidden, g + 1)
                    for k in range(2):
                        ins = pe.transpose(bank(6)[:, k * P:(k + 1) * P], hidden[:, k * P:(k + 1) * P], ident)
                    ins.then_inc(sig.hiddenT_ps, 1)
                    pe.wait_ge(sig.hiddenT, g + 1)
                    pe.wait_ge(sig.out_a, g)
                    pe.wait_ge(sig.out_v, g)
                    arrived(2)
                    for half in range(2):
                        for k in range(2):
                            for j in range(BATCH):
                                w = ring[rd.ring_slot(place, 2, j)][:, :].rearrange("p (c n) -> p c n", c=2)
                                ins = pe.matmul(bank(2 + half)[j * SLOTS:(j + 1) * SLOTS, :],
                                                hiddenT[:, k, j * SLOTS:(j + 1) * SLOTS],
                                                w[:, k, half * HALF:(half + 1) * HALF],
                                                start=(k == 0), stop=(k == 1))
                        if half == 0:
                            ins.then_inc(sig.out_ps, 1)
                        else:
                            ins.then_inc(sig.used, STAGE)
                    pe.wait_ge(sig.scatter, g + 1)
                    for half in range(2):
                        pe.wait_ge((sig.out_a, sig.out_v)[half], g + 1)
                        for t in range(NT):
                            pe.matmul(bank(Y_MOE[t][half]), scatter[:, t * P:(t + 1) * P],
                                      outputs[:, half * HALF:(half + 1) * HALF],
                                      start=True, stop=True).then_inc(sig.y_ps, 1)

                over_batches(pe, batch)

            start_signals(pe, main.by_pe, extra.by_pe)
            pe.sem_inc(extra.used, RING)
            for layer in range(2):
                for t in range(NT):
                    transpose_tokens(2 * layer, t)
                for what, i, part in mixer_order(layer):
                    if what == "slab":
                        slab(layer, i, part)
                    elif what == "turn_heads":
                        turn_heads(layer, i)
                    elif what == "scores":
                        scores(layer, i)
                    elif what == "prob_values":
                        prob_values(layer, i)
                    elif what == "turn_prob":
                        turn_prob(layer, i)
                    elif what == "project_out":
                        project_out(layer, i, 0, part)
                for half in range(2):
                    project_out(layer, OUTS - 1, 0, half)
                for u in range(OUTS):
                    project_out(layer, u, 1, 0)
                transpose_tokens(2 * layer + 1, 0)
                for u in range(OUTS):
                    project_out(layer, u, 1, 1)
                router_logits(layer, 0)
                transpose_tokens(2 * layer + 1, 1)
                router_logits(layer, 1)
                ranks(layer)
                all_rounds(pe, layer, experts, [(extra.used, PER_ROUND)] + per_round(extra.by_pe))

        @block.scalar
        def _(act):
            def square_sum(m, t):
                residual_ready(act, m, t)
                nc.scalar.activation(work3(2 * t), x[:, t, :], ACT.Square,
                                     accum_out=sumsq[:, t:t + 1]).then_inc(s_sq, 1)

            def take_tokT(m, t):
                if m == 0:
                    act.wait_ge(s_first, 48)
                act.wait_ge(s_tokT_ps, 4 * m + 2 * t + 1)
                for c in range(NC // 2):
                    ins = nc.scalar.activation(tokT[:, c, t * P:(t + 1) * P], bank2(2 + 2 * t, 4)[:, c, :], ACT.Copy,
                                               scale=gains[:, m, c:c + 1])
                ins.then_inc(s_tokT_a, 1)

            def before_mixer_or_moe(m):
                square_sum(m, 0)
                take_tokT(m, 0)
                take_tokT(m, 1)
                square_sum(m, 1)

            def slab(layer, s):
                kind, _, col, _ = SLAB_PLAN[layer][s]
                act.wait_ge(s_used, first_unit(layer, "in") + s + 1)
                ps = bank2(6 + s % 2, NT)
                first, cols = (col, ps) if kind == "values" else (512, ps[:, :, 2 * HD:4 * HD])
                if kind in ("values", "shared2"):
                    act.wait_ge(s_rstd, 2 * layer + 1)
                    for t in range(NT):
                        ins = nc.scalar.activation(values[:, t, first:first + cols.shape[-1]], cols[:, t, :],
                                                   ACT.Copy, scale=rstd[:, t:t + 1])
                    ins.then_inc(s_val, 1)
                if kind == "values":
                    return
                i = norm_slabs_before(layer, s)
                w = 2 * HD if kind == "shared2" else 4 * HD
                if i >= 2:
                    act.wait_ge(s_slab, i - 1)
                nc.scalar.activation(square[:, i % 2, 0:NT * w].rearrange("p (t n) -> p t n", t=NT), ps[:, :, 0:w],
                                     ACT.Square).then_inc(s_sqh, 1)

            def take_heads(layer, s):
                i = turns_before(layer, s)
                for (ts, tile, g, part) in TURNS[layer]:
                    if ts != s:
                        continue
                    act.wait_ge(s_hT_ps, i + 1)
                    if i == 0:
                        act.wait_ge(s_prep, 1)
                    scale = 1.0 if layer else head_g[:, g:g + 1]
                    ps = bank2(5, 2)
                    if tile < KEYS:
                        nc.scalar.activation(headsT[:, tile:tile + 2, :], ps, ACT.Copy, scale=scale).then_inc(s_hT, 1)
                    else:
                        act.wait_ge(s_zero, layer + 1)
                        for r in range(2):
                            rows = slice(r * HD, (r + 1) * HD)
                            ins = nc.scalar.activation(headsT[rows, tile + r:tile + 4:2, :], ps[rows, :, :], ACT.Copy,
                                                       scale=1.0 if layer else head_g[rows, g:g + 1])
                        ins.then_inc(s_hT, 1)
                    i += 1

            def exponentials(layer, h):
                g = HEADS * layer + h
                act.wait_ge(s_sc, NT * (g + 1))
                if h >= 2:
                    act.wait_ge(s_pT_ps, g - 1)
                for t in range(NT):
                    src = score[:, h % 2, t, :] if layer == 0 else bank2(h % 2, NT)[:, t, :]
                    ins = nc.scalar.activation(prob[:, h % 2, t, :], src, ACT.Exp, scale=-1.0,
                                               bias=negmax[:, h % 2, t:t + 1], accum_out=rowsum[:, h % 2, t:t + 1])
                if layer == 0 and h >= A_HEADS:
                    k = h - A_HEADS
                    ins = nc.scalar.activation(sink_e[:, h % 2, :], negmax[:, h % 2, :], ACT.Exp,
                                               bias=sink[:, k:k + 1])
                ins.then_inc(s_p, 1)

            def take_probT(layer, h):
                g = HEADS * layer + h
                act.wait_ge(s_pT_ps, g + 1)
                act.wait_ge(s_pv_ps, HEADS // 2 * layer + h // 2)
                nc.scalar.activation(probT[:, h % 2, :, :], bank2(2 + h % 2, NT), ACT.Copy).then_inc(s_pT, 1)

            def take_att(layer, i):
                act.wait_ge(s_pv_ps, HEADS // 2 * layer + i + 1)
                nc.scalar.activation(attT[:, i, :], bank(4)[:, 0:SEQ], ACT.Copy).then_inc(s_att, 1)

            def router(layer):
                act.wait_ge(s_rd, 2 * layer + 1)
                nc.scalar.activation(r_g[:, 5, :, :], r_g[:, 4, :, :], ACT.Exp).then_inc(s_re, 1)
                act.wait_ge(s_rd, 2 * layer + 2)
                nc.scalar.activation(r_s[:, 6, :], r_s[:, 5, :], ACT.Exp).then_inc(s_re, 1)

            def experts(rd, rnd):
                sig = rd.sig

                def batch(step, place):
                    g = rd.batches_before(step, place)
                    act.wait_ge(sig.scatter_ps, g + 1)
                    nc.scalar.activation(scatter, bank(7)[:, 0:SEQ], ACT.Copy).then_inc(sig.scatter, 1)
                    act.wait_ge(sig.used, rd.units_used(step, place, 0))
                    act.wait_ge(sig.hidden, g)
                    nc.scalar.activation(silu, bank(0)[:, 0:DFF], ACT.Silu).then_inc(sig.silu, 1)
                    act.wait_ge(sig.hiddenT_ps, g + 1)
                    nc.scalar.activation(hiddenT, bank2(6, 4)[:, 0:2, :], ACT.Copy).then_inc(sig.hiddenT, 1)
                    act.wait_ge(sig.out_ps, g + 1)
                    nc.scalar.activation(outputs[:, 0:HALF], bank(2), ACT.Copy).then_inc(sig.out_a, 1)

                over_batches(act, batch)

            start_signals(act, main.by_act, extra.by_act)
            for layer in range(2):
                before_mixer_or_moe(2 * layer)
                for what, i, part in mixer_order(layer):
                    if what == "slab" and part == PARTS - 1:
                        slab(layer, i)
                    elif what == "turn_heads":
                        take_heads(layer, i)
                    elif what == "scores":
                        exponentials(layer, i)
                    elif what == "prob_values":
                        take_att(layer, i)
                    elif what == "turn_prob":
                        take_probT(layer, i)
                before_mixer_or_moe(2 * layer + 1)
                router(layer)
                all_rounds(act, layer, experts, per_round(extra.by_act))

        @block.vector
        def _(dve):
            n = [0]
            V = nc.vector

            def link(ins):
                n[0] += 1
                ins.then_inc(s_dve, 1)
                dve.wait_ge(s_dve, n[0])

            def inverse_root(y, v, k):
                half, cube = newton[:, 0, 0:k], newton[:, 1, 0:k]
                link(V.tensor_scalar(half.bitcast(I32), v.bitcast(I32), 1, None, ALU.logical_shift_right))
                link(V.tensor_scalar(y.bitcast(I32), half.bitcast(I32), -1.0, float(0x5f3759df), ALU.mult, ALU.add))
                for _ in range(3):
                    link(V.tensor_tensor(half, y, y, ALU.mult))
                    link(V.scalar_tensor_tensor(cube, half, -0.5, v, ALU.mult, ALU.mult))
                    link(V.scalar_tensor_tensor(y, cube, 1.5, y, ALU.add, ALU.mult))

            def inverse_rms(m):
                dve.wait_ge(s_sq, NT * (m + 1))
                link(V.tensor_scalar(mean[:, :], sumsq[:, :], 1.0 / D, EPS, ALU.mult, ALU.add))
                inverse_root(rstd[:, :], mean[:, :], NT)
                if m % 2 == 0:
                    link(V.tensor_scalar(head_eps[:, :], mean[:, :], HD * EPS, None, ALU.mult))
                dve.sem_inc(s_rstd, 1)

            def normalise_tokens():
                for t in range(NT):
                    V.tensor_scalar(tokens[:, t, :, :], x[:, t, :].rearrange("q (p c) -> q c p", c=NC),
                                    rstd[:, t:t + 1], None, ALU.mult).then_inc(s_tok, 1)

            def take_tokT(m, t):
                if m == 0:
                    dve.wait_ge(s_first, 48)
                dve.wait_ge(s_tokT_ps, 4 * m + 2 * t + 2)
                V.tensor_tensor(tokT[:, NC // 2:NC, t * P:(t + 1) * P], bank2(3 + 2 * t, 4),
                                gains[:, m, NC // 2:NC].unsqueeze(2).to_broadcast([P, NC // 2, P]),
                                ALU.mult).then_inc(s_tokT_v, 1)

            def slab(layer, s):
                kind, _, tile, g = SLAB_PLAN[layer][s]
                if kind == "values":
                    return
                i = norm_slabs_before(layer, s)
                nh = 2 if kind == "shared2" else 4
                w = nh * HD
                ps = bank2(6 + s % 2, NT)[:, :, 0:w].rearrange("p t (h d) -> p t h d", d=HD)
                dve.wait_ge(s_sqh, i + 1)
                link(V.tensor_reduce(head_ss[:, 0:NT * nh],
                                     square[:, i % 2, 0:NT * w].rearrange("p (n d) -> p n d", d=HD), AX, ALU.add))
                sums = head_ss[:, 0:NT * nh].rearrange("p (t h) -> p t h", t=NT)
                link(V.tensor_tensor(sums, sums, head_eps[:, :].unsqueeze(2).to_broadcast([P, NT, nh]), ALU.add))
                inverse_root(head_rs[:, 0:NT * nh], head_ss[:, 0:NT * nh], NT * nh)
                rs = head_rs[:, 0:NT * nh].rearrange("p (t h) -> p t h", t=NT).unsqueeze(3)\
                    .to_broadcast([P, NT, nh, HD])
                if i >= 2:
                    both = kind == "shared4" or SLAB_PLAN[layer][NORMED[i - 1][1]][0] == "shared4"
                    dve.wait_ge(s_hT_ps, turns_before(*NORMED[i if both else i - 1]))
                if layer == 0:
                    dst = normed[:, i % 2, :].rearrange("p (t h d) -> p t h d", t=NT, d=HD)
                    if kind != "shared2":
                        V.tensor_tensor(dst, ps, rs, ALU.mult).then_inc(s_slab, 1)
                    else:
                        dup = normed[:, i % 2, :].rearrange("p (t h r d) -> p t h r d", t=NT, r=2, d=HD)
                        link(V.tensor_tensor(dup[:, :, :, 0, :], ps, rs, ALU.mult))
                        V.tensor_tensor(dup[:, :, :, 1, :], ps, rs, ALU.mult).then_inc(s_slab, 1)
                    return
                flat = square[:, i % 2, :]
                link(V.tensor_tensor(flat.rearrange("p (t h d) -> p t h d", t=NT, d=HD), ps, rs, ALU.mult))

            def rotate(s):
                kind, _, _, g = SLAB_PLAN[1][s]
                if kind == "values":
                    return
                i, w = norm_slabs_before(1, s), 4 * HD
                flat = square[:, i % 2, :]
                tab = 0 if g == "q" else 2
                for t in range(NT):
                    q = flat[:, t * w:(t + 1) * w]
                    r0 = rot[:, 0, t * w:(t + 1) * w]
                    r1 = rot[:, 1, t * w:(t + 1) * w]
                    V.tensor_tensor(r0.rearrange("p (h d) -> p h d", d=HD), q.rearrange("p (h d) -> p h d", d=HD),
                                    rope[:, tab, t, :].unsqueeze(1).to_broadcast([P, 4, HD]), ALU.mult)\
                        .then_inc(s_dve, 1)
                    n[0] += 1

                    def quarter(v, b):
                        return v.rearrange("p (h a b j) -> p h a b j", a=2, b=2, j=16)[:, :, :, b, :]

                    for b in range(2):
                        sin_v = rope[:, tab + 1, t, :].rearrange("p (a b j) -> p a b j", a=2, b=2)[:, :, b, :]
                        V.tensor_tensor(quarter(r1, b), quarter(q, 1 - b),
                                        sin_v.unsqueeze(1).to_broadcast([P, 4, 2, 16]), ALU.mult).then_inc(s_dve, 1)
                        n[0] += 1
                dve.wait_ge(s_dve, n[0])
                if kind == "heads":
                    V.tensor_tensor(normed[:, i % 2, :], rot[:, 0, :], rot[:, 1, :], ALU.add).then_inc(s_slab, 1)
                else:
                    for part in range(2):
                        dst = normed[:, part, :].rearrange("p (t h r d) -> p t h r d", t=NT, r=2, d=HD)
                        for r in range(2):
                            a = [rot[:, k, :].rearrange("p (t n) -> p t n", t=NT)[:, :, part * 2 * HD:(part + 1) * 2 * HD]
                                 .rearrange("p t (h d) -> p t h d", d=HD) for k in range(2)]
                            ins = V.tensor_tensor(dst[:, :, :, r, :], a[0], a[1], ALU.add)
                            if part == 0 or r == 0:
                                link(ins)
                    ins.then_inc(s_slab, 1)

            def maxima(layer, h):
                g = HEADS * layer + h
                dve.wait_ge(s_sc_ps, g + 1)
                b = h % 2
                if layer == 1:
                    V.tensor_reduce(negmax[:, b, :], bank2(b, NT), AX, ALU.min).then_inc(s_sc, NT)
                    return
                if h == 0:
                    dve.wait_ge(s_prep, PREP)
                dve.wait_ge(s_bias, h + 1)
                if h >= 2:
                    dve.wait_ge(s_p, h - 1)
                for t in range(NT):
                    ins = V.tensor_tensor_reduce(score[:, b, t, :], bank2(b, NT)[:, t, :], bias[:, b, t, :],
                                                 1.0, 3.0e38, ALU.add, ALU.min, negmax[:, b, t:t + 1])
                    if h < A_HEADS:
                        ins.then_inc(s_sc, 1)
                    else:
                        link(ins)
                if h >= A_HEADS:
                    k = h - A_HEADS
                    V.tensor_tensor(negmax[:, b, :], negmax[:, b, :], neg_sink[:, k:k + 1].to_broadcast([P, NT]),
                                    ALU.min).then_inc(s_sc, NT)

            def normalise_prob(layer, h):
                g, b = HEADS * layer + h, h % 2
                dve.wait_ge(s_p, g + 1)
                if layer == 0 and h >= A_HEADS:
                    link(V.tensor_tensor(rowsum[:, b, :], rowsum[:, b, :], sink_e[:, b, :], ALU.add))
                link(V.reciprocal(rowinv[:, b, :], rowsum[:, b, :]))
                for t in range(NT):
                    ins = V.tensor_scalar(prob[:, b, t, :], prob[:, b, t, :], rowinv[:, b, t:t + 1], None, ALU.mult)
                ins.then_inc(s_norm, 1)

            def residual(layer, t):
                for half in range(2):
                    if t == 0:
                        dve.wait_ge(s_proj, 2 * layer + 1)
                    elif half == 0:
                        dve.wait_ge(s_proj, 2 * layer + 2)
                    else:
                        dve.wait_ge(s_used, first_unit(layer, "experts"))
                    xs = x[:, t, half * HALF:(half + 1) * HALF]
                    ins = V.tensor_tensor(xs, bank(Y_MIX[t][half]), xs, ALU.add)
                ins.then_inc(s_x0, 1)

            def router(layer):
                G = [r_g[:, i, :, :] for i in range(6)]
                E = [r_e[:, i, :, :] for i in range(8)]
                S = [r_s[:, i, :] for i in range(12)]
                rev4 = cst[:, C_REV4:C_REV4 + GROUPS].unsqueeze(1).to_broadcast([P, NT, GROUPS])
                rev32 = cst[:, C_REV32:C_REV32 + EXPERTS].unsqueeze(1).to_broadcast([P, NT, EXPERTS])

                def over(s, k):
                    return s.unsqueeze(2).to_broadcast([P, NT, k])

                dve.wait_ge(s_rl_ps, NT * (layer + 1))
                for t in range(NT):
                    ins = V.scalar_tensor_tensor(logit[:, t, :], bank(6)[:, t * NR:(t + 1) * NR], rstd[:, t:t + 1],
                                                 router_b[:, layer, :], ALU.mult, ALU.add)
                link(ins)
                lg, le = logit[:, :, 0:GROUPS], logit[:, :, GROUPS:NR]
                link(V.tensor_reduce(S[0], lg, AX, ALU.max))
                V.tensor_tensor(G[4], lg, over(S[0], GROUPS), ALU.subtract).then_inc(s_rd, 1)
                link(V.tensor_tensor(G[0], lg, over(S[0], GROUPS), ALU.is_equal))
                link(V.tensor_tensor(G[1], G[0], rev4, ALU.mult))
                link(V.tensor_reduce(S[1], G[1], AX, ALU.max))
                link(V.tensor_tensor(G[2], G[1], over(S[1], GROUPS), ALU.is_equal))
                link(V.tensor_scalar(G[3], G[2], -1.0, 1.0e37, ALU.add, ALU.mult))
                link(V.tensor_tensor(E[0].rearrange("p t (g e) -> p t g e", g=GROUPS),
                                     le.rearrange("p t (g e) -> p t g e", g=GROUPS),
                                     G[3].unsqueeze(3).to_broadcast([P, NT, GROUPS, PER_GROUP]), ALU.add))

                def best(src, top, onehot):
                    link(V.tensor_reduce(top, src, AX, ALU.max))
                    link(V.tensor_tensor(E[1], src, over(top, EXPERTS), ALU.is_equal))
                    link(V.tensor_tensor(E[2], E[1], rev32, ALU.mult))
                    link(V.tensor_reduce(S[2], E[2], AX, ALU.max))
                    link(V.tensor_tensor(onehot, E[2], over(S[2], EXPERTS), ALU.is_equal))

                best(E[0], S[3], E[3])
                link(V.scalar_tensor_tensor(E[4], E[3], -3.0e37, E[0], ALU.mult, ALU.add))
                best(E[4], S[4], E[5])
                V.tensor_tensor(r_e[:, 7, :, :], E[3], E[5], ALU.add).then_inc(s_pick, 1)
                V.tensor_tensor(S[5], S[4], S[3], ALU.subtract).then_inc(s_rd, 1)
                normalise_tokens()
                dve.wait_ge(s_re, 2 * layer + 2)
                link(V.tensor_reduce(S[7], G[5], AX, ALU.add))
                link(V.tensor_scalar(S[8], S[6], 1.0, None, ALU.add))
                link(V.tensor_tensor(S[9], S[8], S[7], ALU.mult))
                link(V.reciprocal(weight[:, 0, :], S[9]))
                link(V.tensor_tensor(weight[:, 1, :], weight[:, 0, :], S[6], ALU.mult))
                base = cst[:, C_BASE:C_BASE + EXPERTS].unsqueeze(1).to_broadcast([P, NT, EXPERTS])
                for i in range(2):
                    link(V.tensor_tensor(E[6], base, E[3 + 2 * i], ALU.mult))
                    link(V.tensor_reduce(first_slot[:, i, :], E[6], AX, ALU.add))
                dve.wait_ge(s_pos_ps, layer + 1)
                pos = bank(0)[:, 0:NT * EXPERTS].rearrange("p (t e) -> p t e", t=NT)
                for i in range(2):
                    link(V.tensor_tensor(E[6], pos, E[3 + 2 * i], ALU.mult))
                    link(V.tensor_reduce(rank[:, i, :], E[6], AX, ALU.add))

            def largest_count(layer):
                dve.wait_ge(s_count_ps, layer + 1)
                link(V.tensor_reduce(most_f[:, :], bank(1)[0:1, 0:EXPERTS], AX, ALU.max))
                V.tensor_copy(most_i[:, :], most_f[:, :]).then_inc(s_most, 1)

            def experts(rd, rnd):
                sig = rd.sig

                def flat(v):
                    return v.rearrange("p i t -> p (i t)")

                links = [0]

                def then(ins):
                    links[0] += 1
                    ins.then_inc(sig.slots, 1)
                    dve.wait_ge(sig.slots, PER_SLOTS * rounds + links[0])

                rounds = rd.layer if sig is main else (ROUNDS - 1) * rd.layer - 1 + rnd
                if sig is extra:
                    dve.wait_ge(main.chain, 8 * (BATCHES * (rd.layer + 1) + 1))
                if sig is extra or rd.layer:
                    dve.wait_ge(sig.chain, 8 * rd.first)
                if sig is extra:
                    then(V.tensor_scalar(flat(rank[:, :, :]), flat(rank[:, :, :]), -float(SLOTS), None, ALU.add))
                lo, both = flat(inside[:, 0, :, :]), flat(inside[:, 1, :, :])
                fr, fs = flat(rank[:, :, :]), flat(slot[:, :, :])
                if sig is extra:
                    then(V.tensor_scalar(lo, fr, 0.0, None, ALU.is_ge))
                    then(V.scalar_tensor_tensor(both, fr, float(SLOTS), lo, ALU.is_lt, ALU.mult))
                    then(V.tensor_scalar(lo, both, -1.0, 1.0e6, ALU.add, ALU.mult))
                else:
                    V.tensor_scalar(lo, fr, float(SLOTS), 1.0e6, ALU.is_ge, ALU.mult).then_inc(sig.slots, 4)
                    links[0] += 4
                then(V.tensor_tensor(fs, fr, flat(first_slot[:, :, :]), ALU.add))
                V.tensor_tensor(fs, fs, lo, ALU.add).then_inc(sig.slots, 1)
                assert links[0] == PER_SLOTS - 1
                if sig is main:
                    largest_count(rd.layer)

                def batch(step, place):
                    g = rd.batches_before(step, place)
                    dve.wait_ge(sig.slots, PER_SLOTS * (rounds + 1))
                    dve.wait_ge(sig.chain, 8 * g)
                    dve.wait_ge(sig.gather_ps, 2 * g)
                    dve.wait_ge(sig.added, g)
                    for t in range(NT):
                        V.tensor_scalar(onehot[:, 1, t, :], iota, slot[:, 0, t:t + 1], None, ALU.is_equal)\
                            .then_inc(sig.chain, 1)
                    dve.wait_ge(sig.chain, 8 * g + 2)
                    for t in range(NT):
                        ins = V.scalar_tensor_tensor(onehot[:, 0, t, :], iota, slot[:, 1, t:t + 1], onehot[:, 1, t, :],
                                                     ALU.is_equal, ALU.add)
                    ins.then_inc(sig.onehot, 1)
                    dve.wait_ge(sig.scatter_ps, g)
                    dve.wait_ge(sig.onehot, g + 1)
                    for t in range(NT):
                        V.tensor_scalar(onehot[:, 1, t, :], iota, slot[:, 0, t:t + 1], weight[:, 0, t:t + 1],
                                        ALU.is_equal, ALU.mult).then_inc(sig.chain, 1)
                        V.tensor_scalar(weighted2[:, t, :], iota, slot[:, 1, t:t + 1], weight[:, 1, t:t + 1],
                                        ALU.is_equal, ALU.mult).then_inc(sig.chain, 1)
                    dve.wait_ge(sig.chain, 8 * g + 6)
                    V.tensor_tensor(weighted[:, :, :], onehot[:, 1, :, :], weighted2[:, :, :], ALU.add)\
                        .then_inc(sig.weighted, 1)
                    V.tensor_scalar(fs, fs, -float(P), None, ALU.add).then_inc(sig.chain, 2)
                    for h in range(2):
                        dve.wait_ge(sig.gather_ps, 2 * g + h + 1)
                        V.tensor_tensor(gathered[:, 0, 4 * h:4 * h + 4, :], bank2(4 + h, 4),
                                        gains[:, 2 * rd.layer + 1, 4 * h:4 * h + 4].unsqueeze(2)
                                        .to_broadcast([P, 4, P]), ALU.mult).then_inc(sig.gather, 1)
                    dve.wait_ge(sig.used, rd.units_used(step, place, 1))
                    dve.wait_ge(sig.silu, g + 1)
                    V.tensor_tensor(hidden, bank(1)[:, 0:DFF], silu, ALU.mult).then_inc(sig.hidden, 1)
                    dve.wait_ge(sig.used, rd.units_used(step, place, 2))
                    V.tensor_copy(outputs[:, HALF:D], bank(3)).then_inc(sig.out_v, 1)
                    for half in range(2):
                        for t in range(NT):
                            dve.wait_ge(sig.y_ps, 4 * g + 2 * half + t + 1)
                            xs = x[:, t, half * HALF:(half + 1) * HALF]
                            ins = V.tensor_tensor(xs, bank(Y_MOE[t][half]), xs, ALU.add)
                    ins.then_inc(sig.added, 1)

                over_batches(dve, batch)

            start_signals(dve, main.by_dve, extra.by_dve)
            for layer in range(2):
                take_tokT(2 * layer, 0)
                take_tokT(2 * layer, 1)
                inverse_rms(2 * layer)
                for what, i, part in mixer_order(layer):
                    if what == "slab" and part == PARTS - 1:
                        slab(layer, i)
                    elif what == "rotate" and layer == 1:
                        rotate(i)
                    elif what == "scores":
                        if i:
                            normalise_prob(layer, i - 1)
                        maxima(layer, i)
                    elif what == "turn_prob" and i == HEADS - 1:
                        normalise_prob(layer, i)
                residual(layer, 0)
                take_tokT(2 * layer + 1, 0)
                residual(layer, 1)
                take_tokT(2 * layer + 1, 1)
                inverse_rms(2 * layer + 1)
                router(layer)
                all_rounds(dve, layer, experts, [(extra.slots, PER_SLOTS)] + per_round(extra.by_dve))


_INS = ['x', 'mix_norm', 'ffn_norm', 'ab_w_in', 'a_q_norm', 'a_k_norm', 'b_q_norm', 'b_k_norm', 'b_sink',
        'ab_w_out', 'c_w_in', 'c_q_norm', 'c_k_norm', 'c_w_out', 'moe_group_w', 'moe_group_b', 'moe_expert_w',
        'moe_expert_b', 'moe_w_gate', 'moe_w_up', 'moe_w_down']


def kernel(**inputs):
    import concourse.bacc as bacc
    from concourse.bass_utils import run_bass_kernel_spmd

    nc = bacc.Bacc("TRN2", target_bir_lowering=False, num_devices=1)
    arrays, args = {}, []
    for name in _INS + ["shape_constants"]:
        a = shape_constants() if name == "shape_constants" else np.ascontiguousarray(inputs[name])
        arrays[f"in_{name}"] = a
        args.append(nc.dram_tensor(f"in_{name}", a.shape, F32, kind="ExternalInput").ap())
    out = nc.dram_tensor("out_x", (1, SEQ, D), F32, kind="ExternalOutput").ap()
    hybrid_moe_kernel(nc, *args, out)
    r = run_bass_kernel_spmd(nc, [arrays], core_ids=[0])
    return r.results[0]["out_x"]
```
